# Optimizing a Trainium2 kernel written in Bass

```python
import jax, jax.numpy as jnp
from jax import lax
import numpy as np

D_MODEL = 1024
BATCH = 1
SEQ = 512
DEPTH = 2

CONV_GROUPS = 8
CONV_GROUP_DIM = 64
CONV_DIM = CONV_GROUPS * CONV_GROUP_DIM
CONV_WIDTH = 3
GLA_HEADS = 4
GLA_DK = 64
GLA_DV = 128
GLA_RANK = 16
GLA_TAU = 16.0
GLA_CHUNK = 64
SWA_HEADS = 8
SWA_KV_HEADS = 2
SWA_HEAD_DIM = 64
SWA_WINDOW = 128
SWA_BLOCK = 128
ROPE_THETA = 500000.0
ROPE_DIM = SWA_HEAD_DIM // 4
N_BRANCHES = 3
BRANCH_WIDTH = 512
D_FF = 4 * D_MODEL
NORM_EPS = 1e-6
SPLITS = (CONV_DIM, CONV_DIM, CONV_DIM,
          GLA_HEADS * GLA_DK, GLA_HEADS * GLA_DK, GLA_HEADS * GLA_DV, GLA_HEADS * GLA_DV, GLA_RANK,
          SWA_HEADS * SWA_HEAD_DIM, SWA_KV_HEADS * SWA_HEAD_DIM, SWA_KV_HEADS * SWA_HEAD_DIM,
          N_BRANCHES * D_MODEL)
N_IN = sum(SPLITS)

kernel_name = "hybrid_conv_gla_swa_parallel_gated"

def rms_norm(x, w):
    x32 = x.astype(jnp.float32)
    y = x32 * lax.rsqrt(jnp.mean(x32 * x32, axis=-1, keepdims=True) + NORM_EPS)
    return (y * w.astype(jnp.float32)).astype(x.dtype)

def short_conv_mixer(cx, cb, cc, conv_w, conv_b):
    u = cc * cx
    y = lax.conv_general_dilated(
        u, conv_w[:, None, :], window_strides=(1,), padding=[(CONV_WIDTH - 1, 0)],
        dimension_numbers=('NWC', 'WIO', 'NWC'), feature_group_count=CONV_DIM)
    return cb * (y + conv_b)

def gla_mixer(q, k, v, r, a, wa2, ba, onorm_w):
    f32 = jnp.float32
    Bsz, S, _ = q.shape
    N, L = S // GLA_CHUNK, GLA_CHUNK

    def heads(t, d):
        return t.reshape(Bsz, N, L, GLA_HEADS, d).transpose(0, 3, 1, 2, 4)

    q = heads(q.astype(f32) * GLA_DK ** -0.5, GLA_DK)
    k = heads(k.astype(f32), GLA_DK)
    v = heads(v.astype(f32), GLA_DV)
    glog = jax.nn.log_sigmoid((a @ wa2 + ba).astype(f32)) / GLA_TAU
    b = jnp.cumsum(heads(glog, GLA_DK), axis=3)
    b_last = b[:, :, :, -1:, :]
    q_in = q * jnp.exp(b)
    k_in = k * jnp.exp(-b)
    k_end = k * jnp.exp(b_last - b)
    causal = jnp.tril(jnp.ones((L, L), dtype=bool))
    att = jnp.where(causal, jnp.einsum('bhnid,bhnjd->bhnij', q_in, k_in), 0.0)
    o_intra = jnp.einsum('bhnij,bhnjv->bhniv', att, v)
    chunk_kv = jnp.einsum('bhnjd,bhnjv->bhndv', k_end, v)
    chunk_decay = jnp.exp(b_last[:, :, :, 0, :])

    def step(state, inp):
        kv_n, dec_n = inp
        return dec_n[..., None] * state + kv_n, state

    init = jnp.zeros((Bsz, GLA_HEADS, GLA_DK, GLA_DV), f32)
    _, states = lax.scan(step, init, (jnp.moveaxis(chunk_kv, 2, 0), jnp.moveaxis(chunk_decay, 2, 0)))
    states = jnp.moveaxis(states, 0, 2)
    o = o_intra + jnp.einsum('bhnid,bhndv->bhniv', q_in, states)
    o = o.transpose(0, 2, 3, 1, 4).reshape(Bsz, S, GLA_HEADS, GLA_DV)
    o = rms_norm(o, onorm_w).reshape(Bsz, S, GLA_HEADS * GLA_DV)
    return (o * jax.nn.silu(r.astype(f32))).astype(r.dtype)

def rope_partial(x, cos, sin):
    half = ROPE_DIM // 2
    x1, x2, rest = x[..., :half], x[..., half:ROPE_DIM], x[..., ROPE_DIM:]
    return jnp.concatenate([x1 * cos - x2 * sin, x2 * cos + x1 * sin, rest], axis=-1)

def with_prev_block(t):
    pad = ((0, 0), (1, 0)) + ((0, 0),) * (t.ndim - 2)
    prev = jnp.pad(t, pad)[:, :-1]
    return jnp.concatenate([prev, t], axis=2)

def swa_mixer(q, k, v, positions, qn_w, kn_w, sinks):
    f32 = jnp.float32
    Bsz, S, _ = q.shape
    G = SWA_HEADS // SWA_KV_HEADS
    N, T = S // SWA_BLOCK, SWA_BLOCK
    q = rms_norm(q.reshape(Bsz, S, SWA_HEADS, SWA_HEAD_DIM).astype(f32), qn_w)
    k = rms_norm(k.reshape(Bsz, S, SWA_KV_HEADS, SWA_HEAD_DIM).astype(f32), kn_w)
    v = v.reshape(Bsz, S, SWA_KV_HEADS, SWA_HEAD_DIM).astype(f32)
    inv_freq = ROPE_THETA ** (-jnp.arange(0, ROPE_DIM, 2, dtype=f32) / ROPE_DIM)
    ang = positions.astype(f32)[..., None] * inv_freq
    cos, sin = jnp.cos(ang)[:, :, None, :], jnp.sin(ang)[:, :, None, :]
    q = rope_partial(q, cos, sin) * SWA_HEAD_DIM ** -0.5
    k = rope_partial(k, cos, sin)
    qb = q.reshape(Bsz, N, T, SWA_KV_HEADS, G, SWA_HEAD_DIM)
    kw = with_prev_block(k.reshape(Bsz, N, T, SWA_KV_HEADS, SWA_HEAD_DIM))
    vw = with_prev_block(v.reshape(Bsz, N, T, SWA_KV_HEADS, SWA_HEAD_DIM))
    s = jnp.einsum('bnqkgd,bnckd->bkgnqc', qb, kw)
    qpos = jnp.arange(N)[:, None] * T + jnp.arange(T)[None, :]
    kpos = (jnp.arange(N)[:, None] - 1) * T + jnp.arange(2 * T)[None, :]
    diff = qpos[:, :, None] - kpos[:, None, :]
    mask = (diff >= 0) & (diff < SWA_WINDOW) & (kpos[:, None, :] >= 0)
    s = jnp.where(mask, s, -jnp.inf)
    sink = sinks.astype(f32).reshape(SWA_KV_HEADS, G)[None, :, :, None, None, None]
    m = jnp.maximum(jnp.max(s, axis=-1, keepdims=True), sink)
    p = jnp.exp(s - m)
    denom = jnp.sum(p, axis=-1, keepdims=True) + jnp.exp(sink - m)
    o = jnp.einsum('bkgnqc,bnckd->bkgnqd', p, vw) / denom
    o = o.transpose(0, 3, 4, 1, 2, 5).reshape(Bsz, S, SWA_HEADS * SWA_HEAD_DIM)
    return o

def setup_inputs(seed: int = 0) -> dict:
    key = jax.random.key(seed)
    ks = jax.random.split(key, 20)
    f32 = jnp.float32
    nrm = lambda k, shape, scale: jax.random.normal(k, shape, f32) * scale
    x = jax.random.normal(ks[0], (BATCH, SEQ, D_MODEL), f32)
    positions = jnp.broadcast_to(jnp.arange(SEQ, dtype=jnp.int32)[None, :], (BATCH, SEQ))
    return {
        "x": x,
        "positions": positions,
        "norm1_w": 1.0 + nrm(ks[1], (DEPTH, D_MODEL), 0.02),
        "w_in": nrm(ks[2], (DEPTH, D_MODEL, N_IN), D_MODEL ** -0.5),
        "conv_w": nrm(ks[3], (DEPTH, CONV_WIDTH, CONV_DIM), CONV_WIDTH ** -0.5),
        "conv_b": nrm(ks[4], (DEPTH, CONV_DIM), 0.02),
        "gla_wa2": nrm(ks[5], (DEPTH, GLA_RANK, GLA_HEADS * GLA_DK), GLA_RANK ** -0.5),
        "gla_ba": nrm(ks[6], (DEPTH, GLA_HEADS * GLA_DK), 0.1),
        "gla_onorm_w": 1.0 + nrm(ks[7], (DEPTH, GLA_DV), 0.02),
        "q_norm_w": 1.0 + nrm(ks[8], (DEPTH, SWA_HEAD_DIM), 0.02),
        "k_norm_w": 1.0 + nrm(ks[9], (DEPTH, SWA_HEAD_DIM), 0.02),
        "sinks": nrm(ks[10], (DEPTH, SWA_HEADS), 0.5),
        "w_branch": nrm(ks[11], (DEPTH, N_BRANCHES, BRANCH_WIDTH, D_MODEL), BRANCH_WIDTH ** -0.5),
        "w_o": nrm(ks[12], (DEPTH, D_MODEL, D_MODEL), D_MODEL ** -0.5),
        "norm2_w": 1.0 + nrm(ks[13], (DEPTH, D_MODEL), 0.02),
        "w_up": nrm(ks[14], (DEPTH, D_MODEL, D_FF), D_MODEL ** -0.5),
        "w_down": nrm(ks[15], (DEPTH, D_FF, D_MODEL), D_FF ** -0.5),
    }

def reference(x, positions, norm1_w, w_in, conv_w, conv_b, gla_wa2, gla_ba, gla_onorm_w,
              q_norm_w, k_norm_w, sinks, w_branch, w_o, norm2_w, w_up, w_down):
    Bsz, S, D = x.shape
    split_idx = np.cumsum(SPLITS)[:-1].tolist()
    for l in range(DEPTH):
        u = rms_norm(x, norm1_w[l])
        proj = u @ w_in[l]
        (cx, cb, cc, gq, gk, gv, gr, ga, sq, sk, sv, gates) = jnp.split(proj, split_idx, axis=-1)
        ya = short_conv_mixer(cx, cb, cc, conv_w[l], conv_b[l])
        yb = gla_mixer(gq, gk, gv, gr, ga, gla_wa2[l], gla_ba[l], gla_onorm_w[l])
        yc = swa_mixer(sq, sk, sv, positions, q_norm_w[l], k_norm_w[l], sinks[l])
        ybr = jnp.stack([ya.astype(x.dtype), yb.astype(x.dtype), yc.astype(x.dtype)], axis=2)
        branch = jnp.einsum('bsgc,gcd->bsgd', ybr, w_branch[l])
        gate = jax.nn.sigmoid(gates.reshape(Bsz, S, N_BRANCHES, D))
        mixed = jnp.sum(gate * branch, axis=2)
        x = x + mixed @ w_o[l]
        h = rms_norm(x, norm2_w[l])
        x = x + jnp.square(jax.nn.relu(h @ w_up[l])) @ w_down[l]
    return x


_drawn_inputs = setup_inputs


def setup_inputs(seed=0):
    import zlib

    import numpy as np

    out = dict(_drawn_inputs(seed))
    spreads = {}
    factors = {'conv_b': 4.375,
     'gla_ba': 2.973,
     'gla_onorm_w': 6.801,
     'q_norm_w': 8.0,
     'k_norm_w': 8.0,
     'sinks': 56.848}
    for name, (base, spread) in spreads.items():
        noise = np.random.default_rng([zlib.crc32(name.encode()), seed]).standard_normal(out[name].shape)
        drawn = base * np.exp(spread * noise) if base else spread * noise
        out[name] = __import__('jax').numpy.asarray(drawn.astype(out[name].dtype))
    for name, factor in factors.items():
        out[name] = (out[name] * factor).astype(out[name].dtype)
    return out
```

```python
import concourse.bass as bass
from concourse import mybir
from contextlib import ExitStack
import numpy as np

D_MODEL, SEQ, DEPTH = 1024, 512, 2
P = 128
KT = D_MODEL // P
TT = SEQ // P
CONV_DIM, GLA_HEADS, GLA_DK, GLA_DV, GLA_RANK, GLA_CHUNK = 512, 4, 64, 128, 16, 64
SWA_HEADS, SWA_KV, SWA_DIM = 8, 2, 64
N_BRANCH, BRANCH_W, D_FF = 3, 512, 4096
BK = BRANCH_W // P
CHUNKS = SEQ // GLA_CHUNK
EPS = 1e-6
SIZES = dict(cx=CONV_DIM, cb=CONV_DIM, cc=CONV_DIM, gq=256, gk=256, gv=512, gr=512, ga=GLA_RANK,
             sq=512, sk=128, sv=128, gates=N_BRANCH * D_MODEL)
COL = {}
for _name, _n in SIZES.items():
    COL[_name] = sum(SIZES[x] for x in list(SIZES)[:len(COL)])

SLAB_COLS = 256
UNIT_NAMES = (["ga", "void"] + [f"gq{i}" for i in range(2)] + [f"gk{i}" for i in range(2)]
              + [f"gv{i}" for i in range(4)] + [f"sq{i}" for i in range(4)] + ["sk0", "sv0"]
              + [f"cx{i}" for i in range(4)] + [f"cc{i}" for i in range(4)]
              + [f"cb{i}" for i in range(4)] + [f"gr{i}" for i in range(4)])
UNIT = {n: i for i, n in enumerate(UNIT_NAMES)}
PROJ_UNITS = len(UNIT_NAMES)
GATE_IT, MLP_IT = 16, 16
G0 = PROJ_UNITS
O0 = G0 + N_BRANCH * GATE_IT
M0 = O0 + KT
QUARTERS = 4
UNITS = M0 + QUARTERS * MLP_IT
SLABS = PROJ_UNITS // 2 + N_BRANCH * 6 + 4 + QUARTERS * 8
HALF_SLABS = SLABS // 2
SPLIT = 4
AHEAD = 3
GATE_SLAB = [0, 0, 1, 1, 2, 2, 2, 2, 3, 3, 4, 4, 5, 5, 5, 5]

SEQUENCE = """ga gq0 gq1 Z0 gk0 Z1 gk1 X0 X1 gv0 gv1 VT0 KT0 gv2 VT1 KT1 gv3 VT2 ATT0 sq0 VT3 ATT1
sq1 KV0 NS0 sq2 GO0 NS1 sq3 GO1 ATT2 NS2 sk0 ATT3 KV1 NS3 ON0 sv0 NS4 GO2 ON1 cx0 VS0 GO3 ROT4
cx1 ON2 ROT0 cx2 ON3 ROT1 cx3 ROT2 cc0 ROT3 cc1 SC0 cc2 PT0 SC1 cc3 PV0 PT1 SC2 cb0 PV1 PT2 SC3
cb1 PV2 PT3 SC4 cb2 PV3 PT4 SC5 cb3 PV4 PT5 SC6 gr0 PV5 PT6 SC7 gr1 PV6 PT7 gr2 PV7 gr3""".split()


def step_of(word):
    return word.rstrip("0123456789"), int("0" + word[len(word.rstrip("0123456789")):])


FILLS = ["N1"]
for _word in SEQUENCE:
    _kind, _i = step_of(_word)
    if _word in UNIT:
        continue
    if _kind == "KV" or _kind == "SC":
        FILLS += [f"{_word}a", f"{_word}b"]
    elif _kind == "PT":
        FILLS += [f"{_word}cur"] if _i % TT == 0 else [f"{_word}prev", f"{_word}cur"]
    elif _kind != "X":
        FILLS.append(_word)
FILLS.append("N2")
FILL = {n: i for i, n in enumerate(FILLS)}
N_FILLS = len(FILLS)
NORMS = [f for f in FILLS if step_of(f)[0] in ("N", "NS", "ON")]
NORM = {n: i for i, n in enumerate(NORMS)}
N_NORMS = len(NORMS)
XF = KT


def bank_fills(b, before=N_FILLS):
    return sum(1 for i in range(before) if i % 4 == b)


PC = dict(n1=0, n2=8, cw=16, cb=28, ba=32, on=34, qn=35, kn=36, sink=37)
N_PARAMS = 45
CC = dict(ident=0, ones=128, blk=256, rot=384, scan=512, swam=1024, invf=1280)
N_CONST = 1281

TWO_PI = 6.283185307179586
PI_1, PI_2 = 6.28125, 0.001934051513671875
PI_3 = TWO_PI - PI_1 - PI_2
ROUND = 1.5 * 2.0 ** 23


def hybrid_trunk(nc, x, positions, params, w_in, gla_wa2, w_branch, w_o, w_up, w_down, consts, gmask, out):
    f32, f32r, i32 = mybir.dt.float32, mybir.dt.float32r, mybir.dt.int32
    ALU, ACT, AX = mybir.AluOpType, mybir.ActivationFunctionType, mybir.AxisListType
    ctx = ExitStack()
    with ctx:
        TILE = 2048
        BASE = -(-nc.sbuf_base // 64) * 64

        def at(name, tile, shape, dt=f32, extra=0):
            return nc.alloc_sbuf_tensor_at(name, [P] + shape, dt, offset=BASE + tile * TILE + extra)

        xT = at("xT", 0, [KT, SEQ])
        uh = at("uh", 8, [KT, SEQ], f32r)
        ul = at("ul", 16, [KT, SEQ], f32r)
        raw = [at(f"raw{i}", 24 + 4 * i, [KT, SLAB_COLS]) for i in range(2)]
        raw4 = [at(f"raw_branch{i}", 24 + 4 * i, [BK, 2 * SLAB_COLS]) for i in range(2)]
        raw_ga = at("raw_ga", 24, [KT, GLA_RANK])
        wh = [at(f"wh{i}", 32 + 2 * i, [KT, P], f32r) for i in range(SPLIT)]
        wl = [at(f"wl{i}", 40 + 2 * i, [KT, P], f32r) for i in range(SPLIT)]
        yh = at("yh", 48, [12, SEQ], f32r)
        yl = at("yl", 60, [12, SEQ], f32r)
        S = at("gla_states", 48, [2, CHUNKS, P])
        vT = at("gla_v_tokens", 60, [GLA_HEADS, TT, P])
        gq = at("gla_q", 52, [2, SEQ])
        gk = at("gla_k", 54, [2, SEQ])
        kin = at("gla_k_in", 56, [2, SEQ])
        gb = at("gla_b", 58, [2, SEQ])
        eb = at("gla_exp_b", 64, [2, SEQ])
        vtmp = at("v_features", 66, [2, SEQ])
        kendT = at("gla_k_end_tokens", 68, [2, TT, P])
        attm = at("gla_att", 70, [2, TT, P])
        mixed = at("mixed", 72, [KT, SEQ])
        x_tok = at("x_tokens", 72, [TT, D_MODEL])
        cu = at("conv_u", 72, [4, SEQ])
        sm = at("probs", 76, [4, 2 * P])
        pT = at("probs_keys", 78, [2, 4, P])
        yo = at("gla_o", 80, [4, SEQ])
        gt = at("gate_tanh", 80, [4, SEQ])
        sq = at("swa_q", 84, [4, SEQ])
        pos_i = at("positions_i", 84, [SEQ], i32)
        kd = at("swa_k_twice", 88, [2, SEQ])
        vd = at("swa_v_twice", 90, [2, TT, 2, SWA_DIM])
        cosT = at("rope_cos", 92, [SEQ])
        sinT = at("rope_sin", 93, [SEQ])
        ct = at("conv_y", 94, [SEQ])
        T = [at(f"temp{i}", 95 + i, [SEQ]) for i in range(3)]
        nacc = at("norm_sum", 98, [SEQ])
        gaT = at("gla_a", 99, [SEQ])
        cst = at("consts", 100, [N_CONST])
        o = 100 * TILE + 4 * N_CONST
        gm = nc.alloc_sbuf_tensor_at("gla_mask", [P, P], i32, offset=BASE + o + (-o) % 64)
        o = o + (-o) % 64 + 512
        par = nc.alloc_sbuf_tensor_at("params", [P, N_PARAMS], f32, offset=BASE + o)
        o += 192
        wa2 = nc.alloc_sbuf_tensor_at("wa2", [GLA_RANK, 256], f32, offset=BASE + o)
        o += 1024
        small = nc.alloc_sbuf_tensor_at("small", [P, 32], f32, offset=BASE + o)
        ident, ones, blk, rot = (cst[:, CC[n]:CC[n] + P] for n in ("ident", "ones", "blk", "rot"))
        scanm = cst[:, CC["scan"]:CC["scan"] + SEQ]
        swam = cst[:, CC["swam"]:CC["swam"] + 2 * P]
        invf = cst[:, CC["invf"]:CC["invf"] + 1]
        m4, neg4, d4, sum4, es4, den4, qn8 = (small[:, 4 * i:4 * i + 4] for i in range(7))

        acc = [ctx.enter_context(nc.psum_tensor(f"acc{i}", [P, SEQ], f32)) for i in range(4)]
        bank = [ctx.enter_context(nc.psum_tensor(f"bank{i}", [P, SEQ], f32)) for i in range(4)]

        def sem(name):
            return ctx.enter_context(nc.semaphore(name))

        in_full, pos_full, x_full, par_full, out_full = map(sem, "in_full pos_full x_full par_full out_full".split())
        raw_full = [sem(f"raw_full{i}") for i in range(2)]
        raw_free = [sem(f"raw_free{i}") for i in range(2)]
        acc_free = [sem(f"acc_free{i}") for i in range(4)]
        bank_free = [sem(f"bank_free{i}") for i in range(4)]
        (par_free, hi_done, lo_done, unit_done, bank_full, ready0, ga_ready, z_biased, softplus_ready,
         b_ready, gla_exps, gq_ready, gla_qk, gv_ready, sv_ready, vT_ready, kendT_ready, att_ready,
         states_ready, yo_ready, sq_raw, norm_sq, mean_ready, rs_est, rs_used, swa_normed, swa_roped, vs_ready,
         cx_ready, y_val, y_hi, yconv_ready, ygla_ready, gr_tanh, pv_hi, yswa_ready, scores_ready,
         exps_ready, probs_ready, pprev_ready, pcur_ready, gate_ready, gate_used, mixed_done, mx_hi,
         mx_ready, x_upd, x_sq, x_acc, u_val, u_hi, u_ready, relu_ready, hid_val, hid_hi, hid_ready,
         angle_ready, sines_ready, trig_ready, out_copied) = map(sem, """par_free hi_done lo_done
         unit_done bank_full ready0 ga_ready z_biased softplus_ready
         b_ready gla_exps gq_ready gla_qk gv_ready sv_ready vT_ready kendT_ready att_ready
         states_ready yo_ready sq_raw norm_sq mean_ready rs_est rs_used swa_normed swa_roped vs_ready
         cx_ready y_val y_hi yconv_ready ygla_ready gr_tanh pv_hi yswa_ready scores_ready
         exps_ready probs_ready pprev_ready pcur_ready gate_ready gate_used mixed_done mx_hi
         mx_ready x_upd x_sq x_acc u_val u_hi u_ready relu_ready hid_val hid_hi hid_ready
         angle_ready sines_ready trig_ready out_copied""".split())
        UNIT_CREDIT, HID_CREDIT, GATE_CREDIT, XACC_CREDIT = SPLIT, 2, 4, 2

        def unit_index(base, it, pos):
            return it * 16 + (base + pos)

        def slab_half(base, it, pos):
            if base == G0:
                return it * 3 + (G0 // 4 + GATE_SLAB[pos] // 2)
            if base == M0:
                return it * 4 + (19 + pos // 4)
            return (pos // 4) + (17 if base == O0 else 0)

        def slab_slot(base, pos):
            return GATE_SLAB[pos] % 2 if base == G0 else pos // 2 % 2

        def slab_ends(base, pos):
            if base == G0:
                return pos % 16 in (1, 3, 7, 9, 11, 15)
            return pos % 2 == 1

        def k_tiles(base, pos):
            return BK if base == G0 and pos % 8 >= 4 else KT

        def raw_view(base, pos):
            slot = slab_slot(base, pos)
            if base == 0 and pos == 0:
                return raw_ga[:]
            if k_tiles(base, pos) == BK:
                return raw4[slot][:, :, pos % 4 * P:pos % 4 * P + P]
            return raw[slot][:, :, pos % 2 * P:pos % 2 * P + P]

        def split_view(w, base, pos):
            if base == 0 and pos == 0:
                return w[0][:, :, 0:GLA_RANK]
            return w[pos % SPLIT][:, 0:k_tiles(base, pos), :]

        def ahead(base, it, pos):
            pos += AHEAD
            if base == 0 and pos >= PROJ_UNITS:
                return G0, 0, pos - PROJ_UNITS
            if base == G0 and pos >= GATE_IT:
                return G0, it + 1, pos - GATE_IT
            if base == O0 and pos >= KT:
                return M0, 0, pos - KT
            if base == M0 and pos >= MLP_IT:
                return M0, it + 1, pos - MLP_IT
            return base, it, pos

        block = ctx.enter_context(nc.Block())

        @block.sync
        def _(sp):
            sp.dma_start(cst[:], consts).then_inc(in_full, 16)
            sp.dma_start(x_tok[:], x[0].rearrange("(t p) d -> p t d", p=P)).then_inc(x_full, 16)
            sp.dma_start(gm[:], gmask).then_inc(in_full, 16)

            def load(l, base, it, pos, source, into=None):
                slot = slab_slot(base, pos)
                uses = sp.to_reg(l * HALF_SLABS + slab_half(base, it, pos) + 1)
                sp.wait_ge(in_full, 32)
                sp.wait_ge(raw_free[slot], uses)
                sp.dma_start(raw[slot][:] if into is None else into, source).then_inc(raw_full[slot], 16)

            def rows(w, l, first, k, col, n):
                return w[bass.ds(l, 1), first:first + k * P, col:col + n].rearrange(
                    "o (k p) n -> p (o k) n", p=P)

            with sp.Fori(0, DEPTH) as l:
                sp.wait_ge(in_full, 32)
                sp.wait_ge(par_free, l + 1)
                sp.dma_start(par[:], params[bass.ds(l, 1)].rearrange("o p n -> p (o n)")).then_inc(par_full, 16)
                sp.dma_start(wa2[:], gla_wa2[bass.ds(l, 1)].rearrange("o p n -> p (o n)")).then_inc(par_full, 16)
                for pos in range(0, PROJ_UNITS, 2):
                    if pos == 0:
                        load(l, 0, 0, 0, rows(w_in, l, 0, KT, COL["ga"], GLA_RANK), raw_ga[:])
                    else:
                        kind, i = step_of(UNIT_NAMES[pos])
                        load(l, 0, 0, pos, rows(w_in, l, 0, KT, COL[kind] + i * P, SLAB_COLS))
                with sp.Fori(0, N_BRANCH) as g:
                    wg = w_in[bass.ds(l, 1), :, COL["gates"]:].rearrange(
                        "o (k p) (g n) -> p (o k) g n", p=P, g=N_BRANCH)
                    wb = w_branch[bass.ds(l, 1)].rearrange("o g (k p) n -> p (o g) k n", p=P)
                    for half in range(2):
                        for s in range(2):
                            col = 512 * half + SLAB_COLS * s
                            load(l, G0, g, 8 * half + 2 * s, wg[:, :, bass.ds(g, 1), col:col + SLAB_COLS]
                                 .rearrange("p k g n -> p k (g n)"))
                        load(l, G0, g, 8 * half + 4, wb[:, bass.ds(g, 1), :, 512 * half:512 * half + 512]
                             .rearrange("p g k n -> p (g k) n"), raw4[slab_slot(G0, 8 * half + 4)][:])
                for s in range(4):
                    load(l, O0, 0, 2 * s, rows(w_o, l, 0, KT, SLAB_COLS * s, SLAB_COLS))
                with sp.Fori(0, QUARTERS) as q:
                    up = w_up[bass.ds(l, 1)].rearrange("o (k p) (q n) -> p (o k) q n", p=P, q=QUARTERS)
                    down = w_down[bass.ds(l, 1)].rearrange("o (q k p) n -> p (o q) k n", p=P, q=QUARTERS)
                    for s in range(4):
                        load(l, M0, q, 2 * s, up[:, :, bass.ds(q, 1), SLAB_COLS * s:SLAB_COLS * (s + 1)]
                             .rearrange("p k q n -> p k (q n)"))
                    for s in range(4):
                        load(l, M0, q, 8 + 2 * s, down[:, bass.ds(q, 1), :, SLAB_COLS * s:SLAB_COLS * (s + 1)]
                             .rearrange("p q k n -> p (q k) n"))
            for t in range(TT):
                sp.wait_ge(out_copied, 2 * t + 2)
                sp.dma_start(out[0, t * P:(t + 1) * P, :], x_tok[:, t, :]).then_inc(out_full, 16)
            sp.wait_ge(out_full, 16 * TT)

        @block.tensor
        def _(pe):
            pe.sem_inc(unit_done, UNIT_CREDIT)
            pe.wait_ge(ready0, 1)

            def open_bank(l, name, plain=False):
                f = FILL[name]
                uses = pe.to_reg(l * bank_fills(f % 4) + (bank_fills(f % 4, f) + XF // 4 + 1))
                if plain:
                    pe.wait_ge(in_full, 32)
                pe.wait_ge(bank_free[f % 4], uses)
                return bank[f % 4]

            def unit(l, base, it, pos, right_h, right_l, ready=None, ready_at=None, gate=None):
                u = unit_index(base, it, pos)
                pe.wait_ge(lo_done, l * UNITS + u + 1)
                b = (base + pos) % 4
                pe.wait_ge(acc_free[b], l * (UNITS // 4) + it * 4 + (base + pos) // 4 + 1)
                if gate is not None:
                    gate()
                n = k_tiles(base, pos)
                h, lo = split_view(wh, base, pos), split_view(wl, base, pos)
                m = GLA_RANK if base == 0 and pos == 0 else P
                for k in range(n):
                    if ready is not None:
                        pe.wait_ge(ready, ready_at(k))
                    nc.tensor.matmul(acc[b][0:m, :], h[:, k, :], right_h(k), start=k == 0, stop=False)
                    nc.tensor.matmul(acc[b][0:m, :], h[:, k, :], right_l(k), start=False, stop=False)
                    last = nc.tensor.matmul(acc[b][0:m, :], lo[:, k, :], right_h(k), start=False, stop=k == n - 1)
                last.then_inc(unit_done, 2 if base == 0 and pos == 0 else 1)

            def u_tile(t):
                return lambda k: t[:, k, :]

            pe.wait_ge(in_full, 32)
            pe.wait_ge(x_full, 16)
            for k in range(KT):
                pe.wait_ge(bank_free[k % 4], k // 4 + 1)
                for t in range(TT):
                    last = nc.tensor.transpose(bank[k % 4][:, t * P:(t + 1) * P], x_tok[:, t, k * P:(k + 1) * P], ident)
                last.then_inc(bank_full, 1)

            with pe.Fori(0, DEPTH) as l:
                b = open_bank(l, "N1")
                pe.wait_ge(x_acc, l * 16 + XACC_CREDIT + 8)
                nc.tensor.matmul(b[:], ones, nacc[:], start=True, stop=True).then_inc(bank_full, 1)
                for word in SEQUENCE:
                    kind, i = step_of(word)
                    if word in UNIT or word == "ga":
                        pos = UNIT[word]
                        if word == "ga":
                            unit(l, 0, 0, pos, u_tile(uh), u_tile(ul), u_ready, lambda k: l * 16 + k + 1)
                        else:
                            unit(l, 0, 0, pos, u_tile(uh), u_tile(ul))
                    elif kind == "Z":
                        b = open_bank(l, word)
                        pe.wait_ge(ga_ready, l + 1)
                        nc.tensor.matmul(b[:], wa2[:, i * P:(i + 1) * P], gaT[0:GLA_RANK, :],
                                         start=True, stop=True).then_inc(bank_full, 1)
                    elif kind == "VT":
                        b = open_bank(l, word)
                        pe.wait_ge(gv_ready, l * 4 + i + 1)
                        for t in range(TT):
                            last = nc.tensor.transpose(b[:, t * P:(t + 1) * P], vtmp[:, i % 2, t * P:(t + 1) * P], ident)
                        last.then_inc(bank_full, 1)
                    elif kind == "KT":
                        b = open_bank(l, word)
                        pe.wait_ge(gla_qk, l * 2 + i + 1)
                        for t in range(TT):
                            last = nc.tensor.transpose(b[:, t * P:(t + 1) * P], gk[:, i, t * P:(t + 1) * P], ident)
                        last.then_inc(bank_full, 1)
                    elif kind == "ATT":
                        b = open_bank(l, word)
                        pe.wait_ge(gla_qk, l * 2 + i // 2 + 1)
                        r = GLA_DK * (i % 2)
                        for t in range(TT):
                            s = slice(t * P, (t + 1) * P)
                            last = nc.tensor.matmul(b[:, s], kin[r:r + GLA_DK, i // 2, s], gq[r:r + GLA_DK, i // 2, s],
                                                    start=True, stop=True)
                        last.then_inc(bank_full, 1)
                    elif kind == "KV":
                        pe.wait_ge(kendT_ready, l * 2 + i + 1)
                        pe.wait_ge(vT_ready, l * 4 + 2 * i + 2)
                        for odd in range(2):
                            b = open_bank(l, word + "ab"[odd], True)
                            r = GLA_CHUNK * odd
                            for h in range(2):
                                for t in range(TT):
                                    last = nc.tensor.matmul(
                                        b[GLA_DK * h:GLA_DK * (h + 1), t * P:(t + 1) * P],
                                        kendT[r:r + GLA_CHUNK, i, t, GLA_DK * h:GLA_DK * (h + 1)],
                                        vT[r:r + GLA_CHUNK, 2 * i + h, t, :], start=True, stop=True)
                            last.then_inc(bank_full, 1)
                    elif kind == "GO":
                        b = open_bank(l, word)
                        pe.wait_ge(att_ready, l * 4 + i + 1)
                        pe.wait_ge(vT_ready, l * 4 + i + 1)
                        pe.wait_ge(states_ready, l * 2 + i // 2 + 1)
                        r = GLA_DK * (i % 2)
                        for t in range(TT):
                            nc.tensor.matmul(b[:, t * P:(t + 1) * P], vT[:, i, t, :], attm[:, i % 2, t, :],
                                             start=True, stop=False)
                            for c in (2 * t, 2 * t + 1):
                                if c:
                                    s = slice(c * GLA_CHUNK, (c + 1) * GLA_CHUNK)
                                    last = nc.tensor.matmul(b[:, s], S[r:r + GLA_DK, i // 2, c - 1, :],
                                                            gq[r:r + GLA_DK, i // 2, s], start=False,
                                                            stop=c == 2 * t + 1)
                        last.then_inc(bank_full, 1)
                    elif kind in ("NS", "ON"):
                        b = open_bank(l, word)
                        pe.wait_ge(norm_sq, l * (N_NORMS - 2) + NORM[word])
                        nc.tensor.matmul(b[:], blk if kind == "NS" else ones, T[1][:],
                                         start=True, stop=True).then_inc(bank_full, 1)
                    elif kind == "VS":
                        b = open_bank(l, word)
                        pe.wait_ge(sv_ready, l + 1)
                        for t in range(TT):
                            last = nc.tensor.transpose(b[:, t * P:(t + 1) * P], vtmp[:, 0, t * P:(t + 1) * P], ident)
                        last.then_inc(bank_full, 1)
                    elif kind == "ROT":
                        b = open_bank(l, word)
                        pe.wait_ge(swa_normed, l * 5 + i + 1)
                        nc.tensor.matmul(b[:], rot, ct[:] if i == 4 else sq[:, i, :],
                                         start=True, stop=True).then_inc(bank_full, 1)
                    elif kind == "SC":
                        kv, n = i // TT, i % TT
                        pe.wait_ge(swa_roped, l * 5 + 5)
                        for odd in range(2):
                            b = open_bank(l, word + "ab"[odd])
                            r = SWA_DIM * odd
                            first = 0 if n else P
                            for j in range(2):
                                last = nc.tensor.matmul(
                                    b[:, j * 2 * P + first:(j + 1) * 2 * P],
                                    sq[r:r + SWA_DIM, 2 * kv + j, n * P:(n + 1) * P],
                                    kd[r:r + SWA_DIM, kv, (n - 1) * P + first:(n + 1) * P], start=True, stop=True)
                            last.then_inc(bank_full, 1)
                    elif kind == "PT":
                        pe.wait_ge(probs_ready, l * 8 + i + 1)
                        for cur in ((0, 1) if i % TT else (1,)):
                            b = open_bank(l, word + ("cur" if cur else "prev"))
                            for h in range(4):
                                last = nc.tensor.transpose(b[:, h * P:(h + 1) * P], sm[:, h, cur * P:(cur + 1) * P], ident)
                            last.then_inc(bank_full, 1)
                    elif kind == "PV":
                        kv, n = i // TT, i % TT
                        b = open_bank(l, word)
                        pe.wait_ge(vs_ready, l + 1)
                        if n:
                            pe.wait_ge(pprev_ready, l * 6 + kv * 3 + n)
                            nc.tensor.matmul(b[:], vd[:, kv, n - 1].rearrange("p a d -> p (a d)"),
                                             pT[:, 0].rearrange("p h c -> p (h c)"), start=True, stop=False)
                        pe.wait_ge(pcur_ready, l * 8 + i + 1)
                        nc.tensor.matmul(b[:], vd[:, kv, n].rearrange("p a d -> p (a d)"),
                                         pT[:, 1].rearrange("p h c -> p (h c)"), start=n == 0,
                                         stop=True).then_inc(bank_full, 1)
                with pe.Fori(0, N_BRANCH) as g:
                    for pos in range(GATE_IT):
                        if pos % 8 < 4:
                            unit(l, G0, g, pos, u_tile(uh), u_tile(ul))
                        else:
                            def branches_ready():
                                pe.wait_ge(yconv_ready, l * 4 + 4)
                                pe.wait_ge(ygla_ready, l * 4 + 4)
                                pe.wait_ge(yswa_ready, l * 8 + 8)

                            def y_tile(t):
                                return lambda k: t[:, bass.ds(g * BK + k, 1), :].rearrange("p a n -> p (a n)")
                            unit(l, G0, g, pos, y_tile(yh), y_tile(yl), gate=branches_ready if pos == 4 else None)
                for pos in range(KT):
                    if pos == 0:
                        unit(l, O0, 0, pos, u_tile(uh), u_tile(ul), mx_ready, lambda k: l * 8 + k + 1)
                    else:
                        unit(l, O0, 0, pos, u_tile(uh), u_tile(ul))
                b = open_bank(l, "N2")
                pe.wait_ge(x_acc, l * 16 + 8 + XACC_CREDIT + 8)
                nc.tensor.matmul(b[:], ones, nacc[:], start=True, stop=True).then_inc(bank_full, 1)
                with pe.Fori(0, QUARTERS) as q:
                    for pos in range(MLP_IT):
                        if pos == 0:
                            unit(l, M0, q, pos, u_tile(uh), u_tile(ul), u_ready, lambda k: l * 16 + 8 + k + 1)
                        elif pos < 8:
                            unit(l, M0, q, pos, u_tile(uh), u_tile(ul))
                        elif pos == 8:
                            unit(l, M0, q, pos, u_tile(yh), u_tile(yl), hid_ready,
                                 lambda k: l * 32 + q * 8 + k + 1 + HID_CREDIT)
                        else:
                            unit(l, M0, q, pos, u_tile(yh), u_tile(yl))
            pe.wait_ge(x_upd, 8 + 16 * DEPTH)
            for e in range(2 * TT):
                t, half = e // 2, e % 2
                pe.wait_ge(bank_free[e % 4], DEPTH * bank_fills(e % 4) + XF // 4 + e // 4 + 1)
                for j in range(4):
                    last = nc.tensor.transpose(bank[e % 4][:, j * P:(j + 1) * P], xT[:, 4 * half + j, t * P:(t + 1) * P], ident)
                last.then_inc(bank_full, 1)

        @block.scalar
        def _(act):
            act.dma_start(pos_i[:], positions.partition_broadcast(P)).then_inc(pos_full, 16)

            def filled(l, name):
                f = FILL[name]
                act.wait_ge(bank_full, l * N_FILLS + XF + f + 1)
                return bank[f % 4], bank_free[f % 4]

            def split_high(l, base, it, pos):
                act.wait_ge(raw_full[slab_slot(base, pos)], (l * HALF_SLABS + slab_half(base, it, pos)) * 16 + 16)
                act.wait_ge(unit_done, l * UNITS + unit_index(base, it, pos) + 1)
                nc.scalar.activation(split_view(wh, base, pos), raw_view(base, pos), ACT.Copy).then_inc(
                    hi_done, 2 if base == 0 and pos == 0 else 1)

            def done(l, base, it, pos):
                act.wait_ge(unit_done, l * UNITS + unit_index(base, it, pos) + 1 + UNIT_CREDIT)
                return acc[(base + pos) % 4], acc_free[(base + pos) % 4]

            def rsqrt_estimate(l, name):
                act.wait_ge(mean_ready, l * N_NORMS + NORM[name] + 1)
                nc.scalar.activation(T[2][:], T[0][:], ACT.Ln)
                nc.scalar.drain()
                nc.scalar.activation(T[2][:], T[2][:], ACT.Exp, scale=-0.5).then_inc(rs_est, 1)

            one_col = small[:, 29:30]

            def norm_high(l, first):
                for k in range(KT):
                    act.wait_ge(u_val, l * 16 + first + k + 1)
                    nc.scalar.activation(uh[:, k, :], T[k % 2][:], ACT.Copy).then_inc(u_hi, 1)

            act.wait_ge(ready0, 1)
            act.wait_ge(angle_ready, 1)
            nc.scalar.activation(sinT[:], sq[:, 1, :], ACT.Sin)
            nc.scalar.activation(sq[:, 3, :], sq[:, 1, :], ACT.Sin, scale=0.5).then_inc(sines_ready, 1)
            for k in range(KT):
                act.wait_ge(x_upd, k + 1)
                act.wait_ge(x_acc, k + 1)
                nc.scalar.activation(T[k % 2][:], xT[:, k, :], ACT.Square).then_inc(x_sq, 1)

            with act.Fori(0, DEPTH) as l:
                for pos in (0, 2):
                    split_high(l, 0, 0, pos)
                act.wait_ge(rs_used, l * N_NORMS + NORM["N1"] + 1)
                rsqrt_estimate(l, "N1")
                norm_high(l, 0)
                for word in SEQUENCE:
                    kind, i = step_of(word)
                    nc.scalar.drain()
                    if word in UNIT:
                        pos = UNIT[word]
                        split_high(l, *ahead(0, 0, pos))
                        if kind == "ga":
                            split_high(l, *ahead(0, 0, pos + 1))
                        if kind == "gq":
                            a, free = done(l, 0, 0, pos)
                            nc.scalar.activation(gq[:, i, :], a[:], ACT.Copy, scale=GLA_DK ** -0.5).then_inc(free, 1)
                            nc.scalar.drain().then_inc(gq_ready, 1)
                        elif kind in ("gv", "sv"):
                            a, free = done(l, 0, 0, pos)
                            if kind == "gv" and i >= 2:
                                act.wait_ge(bank_full, l * N_FILLS + XF + FILL[f"VT{i - 2}"] + 1)
                            if kind == "sv":
                                act.wait_ge(bank_full, l * N_FILLS + XF + FILL["VT2"] + 1)
                            nc.scalar.activation(vtmp[:, i % 2, :], a[:], ACT.Copy).then_inc(free, 1)
                            nc.scalar.drain().then_inc(gv_ready if kind == "gv" else sv_ready, 1)
                        elif kind == "cx":
                            a, free = done(l, 0, 0, pos)
                            nc.scalar.activation(cu[:, i, :], a[:], ACT.Copy).then_inc(free, 1)
                            nc.scalar.drain().then_inc(cx_ready, 1)
                        elif kind == "cb":
                            act.wait_ge(y_val, l * 8 + i + 1)
                            nc.scalar.activation(yh[:, i, :], T[0][:], ACT.Copy).then_inc(y_hi, 1)
                        elif kind == "gr":
                            a, free = done(l, 0, 0, pos)
                            if i == 0:
                                act.wait_ge(rs_used, l * N_NORMS + NORM["ON3"] + 2)
                            if i >= 2:
                                act.wait_ge(ygla_ready, l * 4 + i - 1)
                            nc.scalar.activation(T[1 + i % 2][:], a[:], ACT.Tanh, scale=0.5).then_inc(gr_tanh, 1)
                            act.wait_ge(y_val, l * 8 + 4 + i + 1)
                            nc.scalar.activation(yh[:, 4 + i, :], T[1 + i % 2][:], ACT.Copy).then_inc(y_hi, 1)
                    elif kind == "Z":
                        act.wait_ge(z_biased, l * 2 + i + 1)
                        nc.scalar.activation(T[1][:], T[0][:], ACT.Abs)
                        nc.scalar.drain()
                        nc.scalar.activation(T[1][:], T[1][:], ACT.Exp, scale=-1.0)
                        nc.scalar.drain()
                        nc.scalar.activation(T[1][:], T[1][:], ACT.Ln, bias=one_col).then_inc(softplus_ready, 1)
                        act.wait_ge(b_ready, l * 2 + i + 1)
                        nc.scalar.activation(eb[:, i, :], gb[:, i, :], ACT.Exp, scale=1.0 / 16)
                        nc.scalar.activation(kin[:, i, :], gb[:, i, :], ACT.Exp, scale=-1.0 / 16)
                        nc.scalar.drain()
                        nc.scalar.activation(gb[:, i, :], T[0][:], ACT.Exp, scale=-1.0 / 16).then_inc(gla_exps, 1)
                    elif kind == "KT":
                        b, free = filled(l, word)
                        nc.scalar.activation(kendT[:, i].rearrange("p t n -> p (t n)"), b[:], ACT.Copy).then_inc(free, 1)
                        nc.scalar.drain().then_inc(kendT_ready, 1)
                    elif kind == "GO":
                        b, free = filled(l, word)
                        nc.scalar.activation(yo[:, i, :], b[:], ACT.Copy).then_inc(free, 1)
                        nc.scalar.drain().then_inc(yo_ready, 1)
                    elif kind in ("NS", "ON"):
                        act.wait_ge(rs_used, l * N_NORMS + NORM[word] + 1)
                        if kind == "NS":
                            act.wait_ge(sq_raw, l * 5 + i + 1)
                            source = ct[:] if i == 4 else sq[:, i, :]
                        else:
                            source = yo[:, i, :]
                        nc.scalar.activation(T[1][:], source, ACT.Square).then_inc(norm_sq, 1)
                        rsqrt_estimate(l, word)
                    elif kind == "SC":
                        act.wait_ge(scores_ready, l * 8 + i + 1)
                        keys = slice(0, 2 * P) if i % TT else slice(P, 2 * P)
                        for h in range(4):
                            nc.scalar.activation(sm[:, h, keys], sm[:, h, keys], ACT.Exp,
                                                 bias=neg4[:, h:h + 1], accum_out=sum4[:, h:h + 1])
                        nc.scalar.activation(es4, d4, ACT.Exp).then_inc(exps_ready, 1)
                    elif kind == "PT":
                        if i % TT:
                            b, free = filled(l, word + "prev")
                            nc.scalar.activation(pT[:, 0].rearrange("p h c -> p (h c)"), b[:], ACT.Copy).then_inc(free, 1)
                            nc.scalar.drain().then_inc(pprev_ready, 1)
                    elif kind == "PV":
                        b, _ = filled(l, word)
                        kv, n = i // TT, i % TT
                        for odd in range(2):
                            r = slice(SWA_DIM * odd, SWA_DIM * (odd + 1))
                            last = nc.scalar.activation(
                                yh[r, 8 + 2 * kv:10 + 2 * kv, n * P:(n + 1) * P],
                                b[r, 2 * odd * P:(2 * odd + 2) * P].rearrange("p (j c) -> p j c", j=2), ACT.Copy)
                        last.then_inc(pv_hi, 1)
                with act.Fori(0, N_BRANCH) as g:
                    for pos in range(GATE_IT):
                        split_high(l, *ahead(G0, g, pos))
                        if pos % 8 < 4:
                            a, free = done(l, G0, g, pos)
                            d = pos // 8 * 4 + pos % 4
                            act.wait_ge(gate_used, l * 24 + g * 8 + (d - 3 + GATE_CREDIT))
                            nc.scalar.activation(gt[:, pos % 4, :], a[:], ACT.Tanh, scale=0.5).then_inc(free, 1)
                            nc.scalar.drain().then_inc(gate_ready, 1)
                act.wait_ge(unit_done, l * UNITS + G0 + 2 * GATE_IT + 12 + UNIT_CREDIT)
                for k in range(KT):
                    act.wait_ge(mixed_done, l * 24 + 16 + k + 1)
                    nc.scalar.activation(uh[:, k, :], mixed[:, k, :], ACT.Copy, scale=0.5).then_inc(mx_hi, 1)
                for pos in range(KT):
                    split_high(l, *ahead(O0, 0, pos))
                    act.wait_ge(x_upd, l * 16 + 8 + pos + 1)
                    act.wait_ge(x_acc, l * 16 + 8 + pos + 1)
                    nc.scalar.activation(T[pos % 2][:], xT[:, pos, :], ACT.Square).then_inc(x_sq, 1)
                act.wait_ge(rs_used, l * N_NORMS + NORM["N2"] + 1)
                rsqrt_estimate(l, "N2")
                norm_high(l, 8)

                def mlp_quarter(q, final):
                    for pos in range(MLP_IT):
                        if not (final and pos + AHEAD >= MLP_IT):
                            split_high(l, *ahead(M0, q, pos))
                        if pos < 8:
                            a, free = done(l, M0, q, pos)
                            act.wait_ge(hid_ready, l * 32 + q * 8 + (pos - 1 + HID_CREDIT))
                            nc.scalar.activation(T[pos % 2][:], a[:], ACT.Relu).then_inc(free, 1)
                            nc.scalar.drain().then_inc(relu_ready, 1)
                            act.wait_ge(hid_val, l * 32 + q * 8 + (pos + 1))
                            nc.scalar.activation(yh[:, pos, :], T[pos % 2][:], ACT.Copy).then_inc(hid_hi, 1)
                        elif final:
                            k = pos - 8
                            act.wait_ge(x_upd, l * 16 + 16 + k + 1)
                            act.wait_ge(x_acc, l * 16 + 16 + k + 1)
                            nc.scalar.activation(T[k % 2][:], xT[:, k, :], ACT.Square).then_inc(x_sq, 1)

                with act.Fori(0, QUARTERS - 1) as q:
                    mlp_quarter(q, False)
                mlp_quarter(QUARTERS - 1, True)

        @block.vector
        def _(dve):
            V = nc.vector
            for s, n in ([(x, 1) for x in raw_free + acc_free + bank_free + [par_free, rs_used]]
                         + [(hid_ready, HID_CREDIT), (gate_used, GATE_CREDIT), (x_acc, XACC_CREDIT)]):
                dve.sem_inc(s, n)
            V.memset(small[:, 29:30], 1.0)
            V.memset(nacc[:], 0.0)
            V.drain().then_inc(ready0, 1)

            def filled(l, name, plain=False):
                f = FILL[name]
                fills = dve.to_reg(l * N_FILLS + (XF + f + 1))
                if plain:
                    dve.wait_ge(in_full, 32)
                dve.wait_ge(bank_full, fills)
                return bank[f % 4], bank_free[f % 4]

            def split_low(l, base, it, pos):
                dve.wait_ge(hi_done, l * UNITS + unit_index(base, it, pos) + (2 if base == 0 and pos == 0 else 1))
                V.tensor_tensor(split_view(wl, base, pos), raw_view(base, pos), split_view(wh, base, pos).bitcast(f32),
                                ALU.subtract).then_inc(lo_done, 2 if base == 0 and pos == 0 else 1)
                if slab_ends(base, pos) or (base == 0 and pos == 0):
                    V.drain().then_inc(raw_free[slab_slot(base, pos)], 1)

            def done(l, base, it, pos):
                dve.wait_ge(unit_done, l * UNITS + unit_index(base, it, pos) + 1 + UNIT_CREDIT)
                return acc[(base + pos) % 4], acc_free[(base + pos) % 4]

            def rsqrt_refine(l, name, n):
                b, free = filled(l, name)
                V.tensor_scalar(T[0][:], b[:], 1.0 / n, EPS, ALU.mult, ALU.add).then_inc(free, 1)
                V.drain().then_inc(mean_ready, 1)
                dve.wait_ge(rs_est, l * N_NORMS + NORM[name] + 1)
                V.tensor_tensor(T[1][:], T[0][:], T[2][:], ALU.mult)
                V.drain()
                V.scalar_tensor_tensor(out=T[1][:], in0=T[1][:], scalar=-0.5, in1=T[2][:], op0=ALU.mult, op1=ALU.mult)
                V.drain()
                V.scalar_tensor_tensor(out=T[2][:], in0=T[1][:], scalar=1.5, in1=T[2][:], op0=ALU.add, op1=ALU.mult)
                V.drain()

            def norm_tiles(l, first, weight):
                def low(k):
                    dve.wait_ge(u_hi, l * 16 + first + k + 1)
                    V.tensor_tensor(ul[:, k, :], T[k % 2][:], uh[:, k, :].bitcast(f32), ALU.subtract).then_inc(u_ready, 1)
                for k in range(KT):
                    V.drain()
                    V.scalar_tensor_tensor(out=T[k % 2][:], in0=xT[:, k, :], scalar=par[:, weight + k:weight + k + 1],
                                           in1=T[2][:], op0=ALU.mult, op1=ALU.mult).then_inc(u_val, 1)
                    if k:
                        low(k - 1)
                low(KT - 1)
                V.drain().then_inc(rs_used, 1)

            dve.wait_ge(in_full, 32)
            dve.wait_ge(pos_full, 16)
            V.tensor_copy(sq[:, 2, :], pos_i[:])
            V.drain()
            V.tensor_scalar(sq[:, 1, :], sq[:, 2, :], invf, None, ALU.mult)
            V.drain()
            V.tensor_scalar(sq[:, 2, :], sq[:, 1, :], 1.0 / TWO_PI, ROUND, ALU.mult, ALU.add)
            V.drain()
            V.tensor_scalar(sq[:, 3, :], sq[:, 2, :], -ROUND, None, ALU.add)
            V.drain()
            for part in (PI_1, PI_2, PI_3):
                V.scalar_tensor_tensor(out=sq[:, 1, :], in0=sq[:, 3, :], scalar=-part, in1=sq[:, 1, :],
                                       op0=ALU.mult, op1=ALU.add)
                V.drain()
            V.tensor_scalar(sq[:, 1, :], sq[:, 1, :], 3.1415925, -3.1415925, ALU.min, ALU.max).then_inc(angle_ready, 1)
            dve.wait_ge(sines_ready, 1)
            V.tensor_tensor(cosT[:], sq[:, 3, :], sq[:, 3, :], ALU.mult)
            V.drain()
            V.tensor_scalar(cosT[:], cosT[:], -2.0, 1.0, ALU.mult, ALU.add)
            for k in range(KT):
                dve.wait_ge(bank_full, k + 1)
                V.tensor_copy(xT[:, k, :], bank[k % 4][:]).then_inc(bank_free[k % 4], 1)
                V.drain().then_inc(x_upd, 1)
                dve.wait_ge(x_sq, k + 1)
                V.tensor_tensor(nacc[:], nacc[:], T[k % 2][:], ALU.add).then_inc(x_acc, 1)
                V.drain()

            with dve.Fori(0, DEPTH) as l:
                for pos in (0, 2):
                    split_low(l, 0, 0, pos)
                dve.wait_ge(par_full, l * 32 + 32)
                rsqrt_refine(l, "N1", D_MODEL)
                norm_tiles(l, 0, PC["n1"])
                V.tensor_scalar(qn8[:, 0:1], par[:, PC["qn"]:PC["qn"] + 1], SWA_DIM ** -0.5, None, ALU.mult)
                for word in SEQUENCE:
                    kind, i = step_of(word)
                    V.drain()
                    if word in UNIT:
                        pos = UNIT[word]
                        split_low(l, *ahead(0, 0, pos))
                        if kind == "ga":
                            a, free = done(l, 0, 0, pos)
                            V.tensor_copy(gaT[0:GLA_RANK, :], a[0:GLA_RANK, :]).then_inc(free, 1)
                            V.drain().then_inc(ga_ready, 1)
                            V.drain().then_inc(acc_free[1], 1)
                            split_low(l, *ahead(0, 0, pos + 1))
                            V.memset(attm[:], 0.0)
                        elif kind == "gk":
                            a, free = done(l, 0, 0, pos)
                            V.tensor_copy(gk[:, i, :], a[:]).then_inc(free, 1)
                        elif kind in ("sq", "sk"):
                            a, free = done(l, 0, 0, pos)
                            V.tensor_copy(ct[:] if kind == "sk" else sq[:, i, :], a[:]).then_inc(free, 1)
                            V.drain().then_inc(sq_raw, 1)
                        elif kind == "cc":
                            dve.wait_ge(cx_ready, l * 4 + i + 1)
                            a, free = done(l, 0, 0, pos)
                            V.tensor_tensor(cu[:, i, :], a[:], cu[:, i, :], ALU.mult).then_inc(free, 1)
                        elif kind == "cb":
                            w = [par[:, PC["cw"] + 4 * k + i:PC["cw"] + 4 * k + i + 1] for k in range(3)]
                            V.drain()
                            V.tensor_scalar(ct[:], cu[:, i, :], w[2], par[:, PC["cb"] + i:PC["cb"] + i + 1], ALU.mult, ALU.add)
                            V.drain()
                            for back in (1, 2):
                                V.scalar_tensor_tensor(out=ct[:, back:], in0=cu[:, i, 0:SEQ - back], scalar=w[2 - back],
                                                       in1=ct[:, back:], op0=ALU.mult, op1=ALU.add)
                                V.drain()
                            a, free = done(l, 0, 0, pos)
                            V.tensor_tensor(T[0][:], a[:], ct[:], ALU.mult).then_inc(free, 1)
                            V.drain().then_inc(y_val, 1)
                            dve.wait_ge(y_hi, l * 8 + i + 1)
                            V.tensor_tensor(yl[:, i, :], T[0][:], yh[:, i, :].bitcast(f32), ALU.subtract).then_inc(yconv_ready, 1)
                        elif kind == "gr":
                            t = T[1 + i % 2]
                            a, free = done(l, 0, 0, pos)
                            dve.wait_ge(gr_tanh, l * 4 + i + 1)
                            V.scalar_tensor_tensor(out=t[:], in0=t[:], scalar=1.0, in1=a[:], op0=ALU.add, op1=ALU.mult).then_inc(free, 1)
                            V.drain()
                            V.scalar_tensor_tensor(out=t[:], in0=t[:], scalar=0.5, in1=yo[:, i, :], op0=ALU.mult,
                                                   op1=ALU.mult).then_inc(y_val, 1)
                            dve.wait_ge(y_hi, l * 8 + 4 + i + 1)
                            V.tensor_tensor(yl[:, 4 + i, :], t[:], yh[:, 4 + i, :].bitcast(f32), ALU.subtract).then_inc(ygla_ready, 1)
                    elif kind == "Z":
                        b, free = filled(l, word)
                        if i:
                            dve.wait_ge(gla_exps, l * 2 + i)
                        V.tensor_scalar(T[0][:], b[:], par[:, PC["ba"] + i:PC["ba"] + i + 1], None, ALU.add).then_inc(free, 1)
                        V.drain().then_inc(z_biased, 1)
                        dve.wait_ge(softplus_ready, l * 2 + i + 1)
                        V.scalar_tensor_tensor(out=T[0][:], in0=T[0][:], scalar=0.0, in1=T[1][:], op0=ALU.min, op1=ALU.subtract)
                        V.drain()
                        V.tensor_tensor_scan(gb[:, i, :], scanm, T[0][:], 0.0, ALU.mult, ALU.add)
                        V.drain()
                        bc = gb[:, i, :].rearrange("p (c n) -> p c n", n=GLA_CHUNK)
                        V.tensor_tensor(T[0][:].rearrange("p (c n) -> p c n", n=GLA_CHUNK), bc,
                                        bc[:, :, GLA_CHUNK - 1:GLA_CHUNK].broadcast_to([P, CHUNKS, GLA_CHUNK]),
                                        ALU.subtract).then_inc(b_ready, 1)
                    elif kind == "X":
                        V.drain()
                        dve.wait_ge(gla_exps, l * 2 + i + 1)
                        dve.wait_ge(gq_ready, l * 2 + i + 1)
                        V.tensor_tensor(gq[:, i, :], gq[:, i, :], eb[:, i, :], ALU.mult)
                        V.tensor_tensor(kin[:, i, :], gk[:, i, :], kin[:, i, :], ALU.mult)
                        V.drain()
                        V.tensor_tensor(gk[:, i, :], gk[:, i, :], gb[:, i, :], ALU.mult).then_inc(gla_qk, 1)
                    elif kind == "VT":
                        b, free = filled(l, word)
                        V.tensor_copy(vT[:, i].rearrange("p t n -> p (t n)"), b[:]).then_inc(free, 1)
                        V.drain().then_inc(vT_ready, 1)
                    elif kind == "ATT":
                        V.drain()
                        if i >= 2:
                            dve.wait_ge(bank_full, l * N_FILLS + XF + FILL[f"GO{i - 2}"] + 1)
                        b, free = filled(l, word, True)
                        for t in range(TT):
                            last = V.copy_predicated(attm[:, i % 2, t, :], gm[:], b[:, t * P:(t + 1) * P])
                        last.then_inc(free, 1)
                        V.drain().then_inc(att_ready, 1)
                    elif kind == "KV":
                        be, free_e = filled(l, word + "a")
                        bo, free_o = filled(l, word + "b")
                        V.tensor_copy(S[:, i, 0, :], be[:, 0:P])
                        for c in range(1, CHUNKS - 1):
                            V.drain()
                            b = (be, bo)[c % 2]
                            last_c = GLA_CHUNK * (c + 1) - 1
                            V.scalar_tensor_tensor(out=S[:, i, c, :], in0=S[:, i, c - 1, :], scalar=eb[:, i, last_c:last_c + 1],
                                                   in1=b[:, c // 2 * P:(c // 2 + 1) * P], op0=ALU.mult, op1=ALU.add)
                        V.drain().then_inc(free_e, 1)
                        V.drain().then_inc(free_o, 1)
                        V.drain().then_inc(states_ready, 1)
                    elif kind == "NS":
                        rsqrt_refine(l, word, SWA_DIM)
                        t = ct[:] if i == 4 else sq[:, i, :]
                        w = par[:, PC["kn"]:PC["kn"] + 1] if i == 4 else qn8[:, 0:1]
                        V.scalar_tensor_tensor(out=t, in0=t, scalar=w, in1=T[2][:], op0=ALU.mult, op1=ALU.mult).then_inc(swa_normed, 1)
                        V.drain().then_inc(rs_used, 1)
                    elif kind == "ON":
                        rsqrt_refine(l, word, GLA_DV)
                        dve.wait_ge(yo_ready, l * 4 + i + 1)
                        V.scalar_tensor_tensor(out=yo[:, i, :], in0=yo[:, i, :], scalar=par[:, PC["on"]:PC["on"] + 1],
                                               in1=T[2][:], op0=ALU.mult, op1=ALU.mult)
                        V.drain().then_inc(rs_used, 1)
                    elif kind == "ROT":
                        V.drain()
                        b, free = filled(l, word)
                        t = ct[:] if i == 4 else sq[:, i, :]
                        V.tensor_tensor(T[0][:], b[:], sinT[:], ALU.mult).then_inc(free, 1)
                        V.tensor_tensor(t, t, cosT[:], ALU.mult)
                        V.drain()
                        if i < 4:
                            V.tensor_tensor(t, t, T[0][:], ALU.add).then_inc(swa_roped, 1)
                        else:
                            V.tensor_tensor(t, t, T[0][:], ALU.add)
                            V.drain()
                            for kv in range(2):
                                for half in range(2):
                                    last = V.tensor_copy(kd[SWA_DIM * half:SWA_DIM * (half + 1), kv, :],
                                                         ct[SWA_DIM * kv:SWA_DIM * (kv + 1), :])
                            V.drain().then_inc(swa_roped, 1)
                    elif kind == "VS":
                        b, free = filled(l, word)
                        bv = b[:].rearrange("p (t k d) -> p t k d", t=TT, k=2)
                        for kv in range(2):
                            for half in range(2):
                                last = V.tensor_copy(vd[:, kv, :, half, :], bv[:, :, kv, :])
                        last.then_inc(free, 1)
                        V.drain().then_inc(vs_ready, 1)
                    elif kind == "SC":
                        first = 0 if i % TT else P
                        width = 2 * P - first
                        if i:
                            dve.wait_ge(bank_full, l * N_FILLS + XF + FILL[f"PT{i - 1}cur"] + 1)
                        for odd in range(2):
                            b, free = filled(l, word + "ab"[odd])
                            V.tensor_tensor(sm[:, 2 * odd:2 * odd + 2, first:], b[:].rearrange("p (j c) -> p j c", j=2)[:, :, first:],
                                            swam.unsqueeze(1).broadcast_to([P, 2, 2 * P])[:, :, first:], ALU.add).then_inc(free, 1)
                        V.drain()
                        V.tensor_reduce(m4, sm[:, :, first:], AX.X, ALU.max)
                        V.drain()
                        sink = par[:, PC["sink"] + i // TT * 4:PC["sink"] + i // TT * 4 + 4]
                        V.tensor_tensor(m4, m4, sink, ALU.max)
                        V.drain()
                        V.tensor_scalar(neg4, m4, -1.0, None, ALU.mult)
                        V.tensor_tensor(d4, sink, m4, ALU.subtract)
                        V.drain().then_inc(scores_ready, 1)
                        dve.wait_ge(exps_ready, l * 8 + i + 1)
                        V.tensor_tensor(den4, sum4, es4, ALU.add)
                        V.drain()
                        V.reciprocal(den4, den4)
                        V.drain()
                        V.tensor_tensor(sm[:, :, first:], sm[:, :, first:],
                                        den4.unsqueeze(2).broadcast_to([P, 4, width]), ALU.mult).then_inc(probs_ready, 1)
                    elif kind == "PT":
                        b, free = filled(l, word + "cur")
                        V.tensor_copy(pT[:, 1].rearrange("p h c -> p (h c)"), b[:]).then_inc(free, 1)
                        V.drain().then_inc(pcur_ready, 1)
                    elif kind == "PV":
                        b, free = filled(l, word)
                        kv, n = i // TT, i % TT
                        dve.wait_ge(pv_hi, l * 8 + i + 1)
                        for odd in range(2):
                            r = slice(SWA_DIM * odd, SWA_DIM * (odd + 1))
                            at_y = (r, slice(8 + 2 * kv, 10 + 2 * kv), slice(n * P, (n + 1) * P))
                            last = V.tensor_tensor(yl[at_y], b[r, 2 * odd * P:(2 * odd + 2) * P].rearrange("p (j c) -> p j c", j=2),
                                                   yh[at_y].bitcast(f32), ALU.subtract)
                        last.then_inc(free, 1)
                        V.drain().then_inc(yswa_ready, 1)
                V.memset(mixed[:], 0.0)
                with dve.Fori(0, N_BRANCH) as g:
                    for pos in range(GATE_IT):
                        V.drain()
                        split_low(l, *ahead(G0, g, pos))
                        if pos % 8 >= 4:
                            d = pos // 8 * 4 + pos % 4
                            dve.wait_ge(gate_ready, l * 24 + g * 8 + (d + 1))
                            a, free = done(l, G0, g, pos)
                            V.scalar_tensor_tensor(out=T[pos % 2][:], in0=gt[:, pos % 4, :], scalar=1.0, in1=a[:],
                                                   op0=ALU.add, op1=ALU.mult).then_inc(free, 1)
                            V.drain().then_inc(gate_used, 1)
                            V.tensor_tensor(mixed[:, d, :], mixed[:, d, :], T[pos % 2][:], ALU.add).then_inc(mixed_done, 1)
                        else:
                            pass
                for k in range(KT):
                    dve.wait_ge(mx_hi, l * 8 + k + 1)
                    V.scalar_tensor_tensor(out=ul[:, k, :], in0=mixed[:, k, :], scalar=0.5, in1=uh[:, k, :].bitcast(f32),
                                           op0=ALU.mult, op1=ALU.subtract).then_inc(mx_ready, 1)
                V.memset(nacc[:], 0.0)

                def add_to_x(base, it, pos, k):
                    a, free = done(l, base, it, pos)
                    V.tensor_tensor(xT[:, k, :], xT[:, k, :], a[:], ALU.add).then_inc(free, 1)

                def add_square(k, n):
                    V.drain().then_inc(x_upd, 1)
                    dve.wait_ge(x_sq, l * 16 + 8 + n + 1)
                    V.tensor_tensor(nacc[:], nacc[:], T[k % 2][:], ALU.add).then_inc(x_acc, 1)
                    V.drain()

                for pos in range(KT):
                    V.drain()
                    split_low(l, *ahead(O0, 0, pos))
                    add_to_x(O0, 0, pos, pos)
                    add_square(pos, pos)
                rsqrt_refine(l, "N2", D_MODEL)
                norm_tiles(l, 8, PC["n2"])
                V.drain().then_inc(par_free, 1)

                def mlp_quarter(q, final):
                    for pos in range(MLP_IT):
                        V.drain()
                        if not (final and pos + AHEAD >= MLP_IT):
                            split_low(l, *ahead(M0, q, pos))
                        if pos < 8:
                            t = T[pos % 2]
                            dve.wait_ge(relu_ready, l * 32 + q * 8 + (pos + 1))
                            V.tensor_tensor(t[:], t[:], t[:], ALU.mult).then_inc(hid_val, 1)
                            dve.wait_ge(hid_hi, l * 32 + q * 8 + (pos + 1))
                            V.tensor_tensor(yl[:, pos, :], t[:], yh[:, pos, :].bitcast(f32), ALU.subtract).then_inc(hid_ready, 1)
                        else:
                            if final and pos == 8:
                                V.memset(nacc[:], 0.0)
                            add_to_x(M0, q, pos, pos - 8)
                            if final:
                                add_square(pos - 8, pos)

                with dve.Fori(0, QUARTERS - 1) as q:
                    mlp_quarter(q, False)
                mlp_quarter(QUARTERS - 1, True)
            for e in range(2 * TT):
                t, half = e // 2, e % 2
                dve.wait_ge(bank_full, DEPTH * N_FILLS + XF + e + 1)
                V.tensor_copy(x_tok[:, t, half * 512:(half + 1) * 512], bank[e % 4][:]).then_inc(bank_free[e % 4], 1)
                V.drain().then_inc(out_copied, 1)


def constants():
    c = np.zeros((P, N_CONST), np.float32)
    p = np.arange(P)
    c[p, CC["ident"] + p] = 1.0
    c[:, CC["ones"]:CC["ones"] + P] = 1.0
    c[:, CC["blk"]:CC["blk"] + P] = p[:, None] // SWA_DIM == p[None, :] // SWA_DIM
    half = SWA_DIM // 4 // 2
    for q in range(P):
        if q % SWA_DIM < half:
            c[q + half, CC["rot"] + q] = -1.0
        elif q % SWA_DIM < 2 * half:
            c[q - half, CC["rot"] + q] = 1.0
    c[:, CC["scan"]:CC["scan"] + SEQ] = np.arange(SEQ) % GLA_CHUNK != 0
    key = np.arange(2 * P)[None, :]
    c[:, CC["swam"]:CC["swam"] + 2 * P] = np.where((key > p[:, None]) & (key <= p[:, None] + P), 0.0, -3.0e38)
    freq = np.float32(500000.0) ** (-np.arange(0, 2 * half, 2, dtype=np.float32) / np.float32(2 * half))
    c[:, CC["invf"]] = np.where(p % SWA_DIM < 2 * half, freq[p % half], 0.0)
    g = (p[None, :] >= p[:, None]) & (p[None, :] // GLA_CHUNK == p[:, None] // GLA_CHUNK)
    return c, g.astype(np.int32)


def kernel(**inputs):
    import concourse.bacc as _bacc
    from concourse.bass_utils import run_bass_kernel_spmd as _run

    a = {k: np.asarray(v) for k, v in inputs.items()}

    def cols(w):
        return w.reshape(DEPTH, -1, P).transpose(0, 2, 1)

    sinks = a["sinks"].reshape(DEPTH, SWA_KV, 2, 2).transpose(0, 1, 3, 2).reshape(DEPTH, 1, SWA_HEADS)
    params = np.concatenate([
        cols(a["norm1_w"]), cols(a["norm2_w"]), cols(a["conv_w"].reshape(DEPTH, -1)), cols(a["conv_b"]),
        cols(a["gla_ba"]), cols(a["gla_onorm_w"]), cols(np.tile(a["q_norm_w"], (1, 2))),
        cols(np.tile(a["k_norm_w"], (1, 2))), np.broadcast_to(sinks, (DEPTH, P, SWA_HEADS))], axis=2)
    consts, gmask = constants()
    feed = dict(x=a["x"], positions=a["positions"][0], params=params, w_in=a["w_in"], gla_wa2=a["gla_wa2"],
                w_branch=a["w_branch"], w_o=a["w_o"], w_up=a["w_up"], w_down=a["w_down"], consts=consts, gmask=gmask)
    nc = _bacc.Bacc("TRN2", target_bir_lowering=False, num_devices=1)
    arrays, args = {}, []
    for name, value in feed.items():
        value = np.ascontiguousarray(value)
        arrays[f"in_{name}_dram"] = value
        args.append(nc.dram_tensor(f"in_{name}_dram", value.shape, mybir.dt.from_np(value.dtype), kind="ExternalInput").ap())
    args.append(nc.dram_tensor("out_0_dram", (1, SEQ, D_MODEL), mybir.dt.float32, kind="ExternalOutput").ap())
    hybrid_trunk(nc, *args)
    r = _run(nc, [arrays], core_ids=[0])
    return r.results[0]["out_0_dram"]
```

```python
import concourse.bass as bass
from concourse import mybir
from contextlib import ExitStack
import numpy as np

D_MODEL, SEQ, DEPTH = 1024, 512, 2
P = 128
KT = D_MODEL // P
TT = SEQ // P
CONV_DIM, GLA_HEADS, GLA_DK, GLA_DV, GLA_RANK, GLA_CHUNK = 512, 4, 64, 128, 16, 64
SWA_HEADS, SWA_KV, SWA_DIM = 8, 2, 64
N_BRANCH, BRANCH_W, D_FF = 3, 512, 4096
BK = BRANCH_W // P
CHUNKS = SEQ // GLA_CHUNK
EPS = 1e-6
SIZES = dict(cx=CONV_DIM, cb=CONV_DIM, cc=CONV_DIM, gq=256, gk=256, gv=512, gr=512, ga=GLA_RANK,
             sq=512, sk=128, sv=128, gates=N_BRANCH * D_MODEL)
COL = {}
for _name, _n in SIZES.items():
    COL[_name] = sum(SIZES[x] for x in list(SIZES)[:len(COL)])

SLAB_COLS = 256
UNIT_NAMES = (["ga", "void"] + [f"gq{i}" for i in range(2)] + [f"gk{i}" for i in range(2)]
              + [f"gv{i}" for i in range(4)] + [f"sq{i}" for i in range(4)] + ["sk0", "sv0"]
              + [f"cx{i}" for i in range(4)] + [f"cc{i}" for i in range(4)]
              + [f"cb{i}" for i in range(4)] + [f"gr{i}" for i in range(4)])
UNIT = {n: i for i, n in enumerate(UNIT_NAMES)}
PROJ_UNITS = len(UNIT_NAMES)
GATE_IT, MLP_IT = 16, 16
G0 = PROJ_UNITS
O0 = G0 + N_BRANCH * GATE_IT
M0 = O0 + KT
QUARTERS = 4
UNITS = M0 + QUARTERS * MLP_IT
SLABS = PROJ_UNITS // 2 + N_BRANCH * 6 + 4 + QUARTERS * 8
HALF_SLABS = SLABS // 2
SPLIT = 4
AHEAD = 3
GATE_SLAB = [0, 0, 1, 1, 2, 2, 2, 2, 3, 3, 4, 4, 5, 5, 5, 5]

SEQUENCE = """ga NSUM gq0 NROW gq1 ZA gk0 ZB gk1 gv0 gv1 VT0 X0 X1 gv2 VT1 KT0 KT1 gv3 VT2 ATT0 sq0 VT3 ATT1
sq1 KV0 sq2 GO0 GO1 sq3 ATT2 ATT3 sk0 KV1 sv0 QSUM cx0 VS0 GO2 GO3 cx1 QN4 QN0 cx2 QN1 OSUM
cx3 SC0 QN2 cc0 ON0 QN3 SM0 SC1 cc1 PT0 SM1 SC2 ON1 cc2 PV0 PT1 SM2 SC3 cc3 PV1 PT2 SM3 SC4 ON2
cb0 PV2 PT3 SM4 SC5 ON3 cb1 PV3 PT4 SM5 SC6 cb2 PV4 PT5 SM6 SC7 cb3 PV5 PT6 SM7 gr0 PV6 PT7 gr1 PV7 gr2 gr3""".split()


def step_of(word):
    return word.rstrip("0123456789"), int("0" + word[len(word.rstrip("0123456789")):])


FILLS = []
for _word in SEQUENCE:
    _kind, _i = step_of(_word)
    if _word in UNIT:
        continue
    if _kind in ("KV", "SC", "ZA"):
        FILLS += [f"{_word}a", f"{_word}b"]
    elif _kind == "PT":
        FILLS += [f"{_word}cur"] if _i % TT == 0 else [f"{_word}prev", f"{_word}cur"]
    elif _kind not in ("X", "ZB", "SM"):
        FILLS.append(_word)
FILLS += ["NSUM2", "NROW2"]
FILL = {n: i for i, n in enumerate(FILLS)}
N_FILLS = len(FILLS)
XF = KT


def bank_fills(b, before=N_FILLS):
    return sum(1 for i in range(before) if i % 4 == b)


PC = dict(cw=0, cb=12, ba=16, on=18, qn=19, kn=20, sink=21)
N_PARAMS = 29
CC = dict(ident=0, scan=128, swam=640, invf=896, ones=897, blk=898, sign=900)
N_CONST = 901
HEADS_Q = SWA_HEADS + SWA_KV

ROPE_HALF = SWA_DIM // 4 // 2
ROPE_SWAP = [(i + ROPE_HALF) % (2 * ROPE_HALF) if i < 2 * ROPE_HALF else i for i in range(32)]

TWO_PI = 6.283185307179586
PI_1, PI_2 = 6.28125, 0.001934051513671875
PI_3 = TWO_PI - PI_1 - PI_2
ROUND = 1.5 * 2.0 ** 23


def hybrid_trunk(nc, x, positions, params, w_in, gla_wa2, w_branch, w_o, w_up, w_down, norms, consts, gmask, out):
    f32, f32r, i32 = mybir.dt.float32, mybir.dt.float32r, mybir.dt.int32
    ALU, ACT, AX = mybir.AluOpType, mybir.ActivationFunctionType, mybir.AxisListType
    ctx = ExitStack()
    with ctx:
        TILE = 2048
        BASE = -(-nc.sbuf_base // 64) * 64

        def at(name, tile, shape, dt=f32, extra=0):
            return nc.alloc_sbuf_tensor_at(name, [P] + shape, dt, offset=BASE + tile * TILE + extra)

        xT = at("xT", 0, [KT, SEQ])
        uh = at("uh", 8, [KT, SEQ], f32r)
        ul = at("ul", 16, [KT, SEQ], f32r)
        raw = [at(f"raw{i}", 24 + 4 * i, [KT, SLAB_COLS]) for i in range(2)]
        raw4 = [at(f"raw_branch{i}", 24 + 4 * i, [BK, 2 * SLAB_COLS]) for i in range(2)]
        raw_ga = at("raw_ga", 24, [KT, GLA_RANK])
        wh = [at(f"wh{i}", 32 + 2 * i, [KT, P], f32r) for i in range(SPLIT)]
        wl = [at(f"wl{i}", 40 + 2 * i, [KT, P], f32r) for i in range(SPLIT)]
        yh = at("yh", 48, [12, SEQ], f32r)
        yl = at("yl", 60, [12, SEQ], f32r)
        S = at("gla_states", 48, [2, CHUNKS, P])
        vT = at("gla_v_tokens", 60, [GLA_HEADS, TT, P])
        gq = at("gla_q", 52, [2, SEQ])
        gk = at("gla_k", 54, [2, SEQ])
        kin = at("gla_k_in", 56, [2, SEQ])
        gb = at("gla_b", 58, [2, SEQ])
        eb = at("gla_exp_b", 64, [2, SEQ])
        vtmp = at("v_features", 66, [2, SEQ])
        kendT = at("gla_k_end_tokens", 68, [2, TT, P])
        attm = at("gla_att", 70, [2, TT, P])
        mixed = at("mixed", 72, [KT, SEQ])
        x_tok = at("x_tokens", 72, [TT, D_MODEL])
        cu = at("conv_u", 72, [4, SEQ])
        sm = [at(f"probs{i}", (52, 76)[i], [4, 2 * P]) for i in range(2)]
        pT = at("probs_keys", 78, [2, 4, P])
        yo = at("gla_o", 80, [4, SEQ])
        gt = at("gate_tanh", 80, [4, SEQ])
        sq = at("swa_q", 84, [4, SEQ])
        pos_i = at("positions_i", 84, [SEQ], i32)
        kd = at("swa_k_twice", 88, [2, SEQ])
        vd = at("swa_v_twice", 90, [2, TT, 2, SWA_DIM])
        cosT = at("rope_cos", 92, [SEQ])
        sinT = at("rope_sin", 93, [SEQ])
        ct = at("conv_y", 94, [SEQ])
        T3 = at("temps", 95, [3, SEQ])
        T = [T3[:, i, :] for i in range(3)]
        rs_sq = T[2]
        nacc = at("norm_sum", 98, [SEQ])
        rs = at("rsqrt_rows", 99, [SEQ])
        gaT = at("gla_a", 64, [SEQ])
        rs2 = at("rsqrt_rows_mlp", 94, [SEQ])
        sqr = at("squares", 76, [4, SEQ])
        sqk = at("squares_k", 98, [SEQ])
        sqo = at("squares_o", 54, [4, SEQ])
        cst = at("consts", 100, [N_CONST])
        o = 100 * TILE + 4 * N_CONST
        gm = nc.alloc_sbuf_tensor_at("gla_mask", [P, P], i32, offset=BASE + o + (-o) % 64)
        o = o + (-o) % 64 + 512
        par = nc.alloc_sbuf_tensor_at("params", [P, N_PARAMS], f32, offset=BASE + o)
        o += 192
        wa2 = nc.alloc_sbuf_tensor_at("wa2", [GLA_RANK, 256], f32, offset=BASE + o)
        o += 1024
        small = nc.alloc_sbuf_tensor_at("small", [P, 64], f32, offset=BASE + o)
        o += 256
        nw = nc.alloc_sbuf_tensor_at("norm_weights", [P, 2 * DEPTH * KT], f32, offset=BASE + o)
        o += 128
        stat = nc.alloc_sbuf_tensor_at("stat", [P, 4, TT * HEADS_Q], f32, offset=BASE + o)
        o += 16 * TT * HEADS_Q
        stat_i = nc.alloc_sbuf_tensor_at("stat_bits", [P, TT * HEADS_Q], i32, offset=BASE + o)
        ident, ones, blk = cst[:, 0:P], cst[:, CC["ones"]:CC["ones"] + 1], cst[:, CC["blk"]:CC["blk"] + 2]
        scanm = cst[:, CC["scan"]:CC["scan"] + SEQ]
        swam = cst[:, CC["swam"]:CC["swam"] + 2 * P]
        invf, sign = cst[:, CC["invf"]:CC["invf"] + 1], cst[:, CC["sign"]:CC["sign"] + 1]
        neg4, d4, sum4, es4, den4 = ([small[:, 8 * i + 4 * j:8 * i + 4 * j + 4] for j in range(2)] for i in range(5))
        m4, qn8, one_col = small[:, 40:44], small[:, 44:45], small[:, 45:46]

        acc = [ctx.enter_context(nc.psum_tensor(f"acc{i}", [P, SEQ], f32)) for i in range(4)]
        bank = [ctx.enter_context(nc.psum_tensor(f"bank{i}", [P, SEQ], f32)) for i in range(4)]

        def sem(name):
            return ctx.enter_context(nc.semaphore(name))

        in_full, pos_full, gm_full, nw_full, par_full, out_full = map(
            sem, "in_full pos_full gm_full nw_full par_full out_full".split())
        x_full = [sem(f"x_full{i}") for i in range(TT)]
        raw_full = [sem(f"raw_full{i}") for i in range(2)]
        raw_free = [sem(f"raw_free{i}") for i in range(2)]
        acc_free = [sem(f"acc_free{i}") for i in range(4)]
        bank_free = [sem(f"bank_free{i}") for i in range(4)]
        (par_free, hi_done, lo_done, unit_done, bank_full, ready0, ga_ready, z_biased, softplus_ready,
         b_ready, gla_exps, gla_qk, gv_ready, sv_ready, vT_ready, kendT_ready, att_ready,
         states_ready, yo_ready, yo_sq, swa_raw, swa_sq, stat_ready, swa_roped, vs_ready, y_val,
         y_hi, yconv_ready, ygla_ready, gr_scaled, gr_tanh, pv_hi, yswa_ready, scores_ready, exps_ready, den_ready,
         probs_ready, pprev_ready, pcur_ready, gate_scaled, gate_ready, mixed_done, mx_hi, mx_ready, x_upd,
         x_sq, x_acc, u_hi, u_ready, relu_ready, hid_val, hid_hi, hid_ready, angle_ready, sines_ready,
         out_copied) = map(sem, """
         par_free hi_done lo_done unit_done bank_full ready0 ga_ready z_biased softplus_ready b_ready
         gla_exps gla_qk gv_ready sv_ready vT_ready kendT_ready att_ready states_ready yo_ready
         yo_sq swa_raw swa_sq stat_ready swa_roped vs_ready y_val y_hi yconv_ready ygla_ready
         gr_scaled gr_tanh pv_hi yswa_ready scores_ready exps_ready den_ready probs_ready pprev_ready pcur_ready
         gate_scaled gate_ready mixed_done mx_hi mx_ready x_upd x_sq x_acc u_hi u_ready relu_ready hid_val
         hid_hi hid_ready angle_ready sines_ready out_copied""".split())
        UNIT_CREDIT, HID_CREDIT = SPLIT, 2

        def unit_index(base, it, pos):
            return it * 16 + (base + pos)

        def slab_half(base, it, pos):
            if base == G0:
                return it * 3 + (G0 // 4 + GATE_SLAB[pos] // 2)
            if base == M0:
                return it * 4 + (19 + pos // 4)
            return (pos // 4) + (17 if base == O0 else 0)

        def slab_slot(base, pos):
            return GATE_SLAB[pos] % 2 if base == G0 else pos // 2 % 2

        def slab_ends(base, pos):
            if base == G0:
                return pos % 16 in (1, 3, 7, 9, 11, 15)
            return pos % 2 == 1

        def k_tiles(base, pos):
            return BK if base == G0 and pos % 8 >= 4 else KT

        def raw_view(base, pos):
            slot = slab_slot(base, pos)
            if base == 0 and pos == 0:
                return raw_ga[:]
            if k_tiles(base, pos) == BK:
                return raw4[slot][:, :, pos % 4 * P:pos % 4 * P + P]
            return raw[slot][:, :, pos % 2 * P:pos % 2 * P + P]

        def split_view(w, base, pos):
            if base == 0 and pos == 0:
                return w[0][:, :, 0:GLA_RANK]
            return w[pos % SPLIT][:, 0:k_tiles(base, pos), :]

        def ahead(base, it, pos):
            pos += AHEAD
            if base == 0 and pos >= PROJ_UNITS:
                return G0, 0, pos - PROJ_UNITS
            if base == G0 and pos >= GATE_IT:
                return G0, it + 1, pos - GATE_IT
            if base == O0 and pos >= KT:
                return M0, 0, pos - KT
            if base == M0 and pos >= MLP_IT:
                return M0, it + 1, pos - MLP_IT
            return base, it, pos

        block = ctx.enter_context(nc.Block())

        @block.sync
        def _(sp):
            sp.dma_start(cst[:], consts).then_inc(in_full, 16)
            for t in range(TT):
                sp.dma_start(x_tok[:, t, :], x[0, t * P:(t + 1) * P, :]).then_inc(x_full[t], 16)

            def load(l, base, it, pos, source, into=None):
                slot = slab_slot(base, pos)
                uses = sp.to_reg(l * HALF_SLABS + slab_half(base, it, pos) + 1)
                sp.wait_ge(in_full, 16)
                sp.wait_ge(raw_free[slot], uses)
                sp.dma_start(raw[slot][:] if into is None else into, source).then_inc(raw_full[slot], 16)

            def rows(w, l, first, k, col, n):
                return w[bass.ds(l, 1), first:first + k * P, col:col + n].rearrange(
                    "o (k p) n -> p (o k) n", p=P)

            with sp.Fori(0, DEPTH) as l:
                sp.wait_ge(in_full, 16)
                sp.wait_ge(par_free, l + 1)
                sp.dma_start(par[:], params[bass.ds(l, 1)].rearrange("o p n -> p (o n)")).then_inc(par_full, 16)
                sp.dma_start(wa2[:], gla_wa2[bass.ds(l, 1)].rearrange("o p n -> p (o n)")).then_inc(par_full, 16)
                for pos in range(0, PROJ_UNITS, 2):
                    if pos == 0:
                        load(l, 0, 0, 0, rows(w_in, l, 0, KT, COL["ga"], GLA_RANK), raw_ga[:])
                    else:
                        kind, i = step_of(UNIT_NAMES[pos])
                        load(l, 0, 0, pos, rows(w_in, l, 0, KT, COL[kind] + i * P, SLAB_COLS))
                with sp.Fori(0, N_BRANCH) as g:
                    wg = w_in[bass.ds(l, 1), :, COL["gates"]:].rearrange(
                        "o (k p) (g n) -> p (o k) g n", p=P, g=N_BRANCH)
                    wb = w_branch[bass.ds(l, 1)].rearrange("o g (k p) n -> p (o g) k n", p=P)
                    for half in range(2):
                        for s in range(2):
                            col = 512 * half + SLAB_COLS * s
                            load(l, G0, g, 8 * half + 2 * s, wg[:, :, bass.ds(g, 1), col:col + SLAB_COLS]
                                 .rearrange("p k g n -> p k (g n)"))
                        load(l, G0, g, 8 * half + 4, wb[:, bass.ds(g, 1), :, 512 * half:512 * half + 512]
                             .rearrange("p g k n -> p (g k) n"), raw4[slab_slot(G0, 8 * half + 4)][:])
                for s in range(4):
                    load(l, O0, 0, 2 * s, rows(w_o, l, 0, KT, SLAB_COLS * s, SLAB_COLS))
                with sp.Fori(0, QUARTERS) as q:
                    up = w_up[bass.ds(l, 1)].rearrange("o (k p) (q n) -> p (o k) q n", p=P, q=QUARTERS)
                    down = w_down[bass.ds(l, 1)].rearrange("o (q k p) n -> p (o q) k n", p=P, q=QUARTERS)
                    for s in range(4):
                        load(l, M0, q, 2 * s, up[:, :, bass.ds(q, 1), SLAB_COLS * s:SLAB_COLS * (s + 1)]
                             .rearrange("p k q n -> p k (q n)"))
                    for s in range(4):
                        load(l, M0, q, 8 + 2 * s, down[:, bass.ds(q, 1), :, SLAB_COLS * s:SLAB_COLS * (s + 1)]
                             .rearrange("p q k n -> p (q k) n"))
            for t in range(TT):
                sp.wait_ge(out_copied, 2 * t + 2)
                sp.dma_start(out[0, t * P:(t + 1) * P, :], x_tok[:, t, :]).then_inc(out_full, 16)
            sp.wait_ge(out_full, 16 * TT)

        @block.tensor
        def _(pe):
            pe.sem_inc(unit_done, UNIT_CREDIT)
            pe.wait_ge(ready0, 1)

            def open_bank(l, name, plain=False):
                f = FILL[name]
                uses = pe.to_reg(l * bank_fills(f % 4) + (bank_fills(f % 4, f) + XF // 4 + 1))
                if plain:
                    pe.wait_ge(in_full, 16)
                pe.wait_ge(bank_free[f % 4], uses)
                return bank[f % 4]

            def unit(l, base, it, pos, right_h, right_l, ready=None, ready_at=None, gate=None):
                u = unit_index(base, it, pos)
                pe.wait_ge(lo_done, l * UNITS + u + 1)
                b = (base + pos) % 4
                pe.wait_ge(acc_free[b], l * (UNITS // 4) + it * 4 + (base + pos) // 4 + 1)
                if gate is not None:
                    gate()
                n = k_tiles(base, pos)
                h, lo = split_view(wh, base, pos), split_view(wl, base, pos)
                m = GLA_RANK if base == 0 and pos == 0 else P
                for k in range(n):
                    if ready is not None:
                        pe.wait_ge(ready, ready_at(k))
                    nc.tensor.matmul(acc[b][0:m, :], h[:, k, :], right_h(k), start=k == 0, stop=False)
                    nc.tensor.matmul(acc[b][0:m, :], h[:, k, :], right_l(k), start=False, stop=False)
                    last = nc.tensor.matmul(acc[b][0:m, :], lo[:, k, :], right_h(k), start=False, stop=k == n - 1)
                last.then_inc(unit_done, 2 if base == 0 and pos == 0 else 1)

            def u_tile(t):
                return lambda k: t[:, k, :]

            pe.wait_ge(in_full, 16)
            for t in range(TT):
                pe.wait_ge(x_full[t], 16)
            for k in range(KT):
                pe.wait_ge(bank_free[k % 4], k // 4 + 1)
                for t in range(TT):
                    last = nc.tensor.transpose(bank[k % 4][:, t * P:(t + 1) * P], x_tok[:, t, k * P:(k + 1) * P], ident)
                last.then_inc(bank_full, 1)

            def sum_squares(l, name, first):
                b = open_bank(l, name)
                pe.wait_ge(x_acc, l * 16 + first + 8)
                for t in range(TT):
                    last = nc.tensor.matmul(b[:, t:t + 1], nacc[:, t * P:(t + 1) * P], ones, start=True, stop=True)
                last.then_inc(bank_full, 1)

            def rows(l, name, ready_at, result, columns):
                b = open_bank(l, name)
                pe.wait_ge(stat_ready, l * 4 + ready_at)
                m = P // len(columns(0))
                for t in range(TT):
                    for j, c in enumerate(columns(t)):
                        into, column = b[m * j:m * (j + 1), t * P:(t + 1) * P], stat[:, result, c:c + 1].broadcast_to([P, m])
                        if m == P:
                            last = nc.tensor.transpose(into, column, ident)
                        else:
                            last = nc.tensor.matmul(into, column, ident, start=True, stop=True)
                last.then_inc(bank_full, 1)

            with pe.Fori(0, DEPTH) as l:
                for word in SEQUENCE:
                    kind, i = step_of(word)
                    if word in UNIT or word == "ga":
                        pos = UNIT[word]
                        if word == "ga":
                            unit(l, 0, 0, pos, u_tile(uh), u_tile(ul), u_ready, lambda k: l * 16 + k + 1)
                        else:
                            unit(l, 0, 0, pos, u_tile(uh), u_tile(ul))
                    elif kind == "NSUM":
                        sum_squares(l, word, 0)
                    elif kind == "NROW":
                        rows(l, word, 1, 1, lambda t: [t])
                    elif kind == "ZA":
                        for pair in range(2):
                            b = open_bank(l, word + "ab"[pair])
                            pe.wait_ge(ga_ready, l + 1)
                            nc.tensor.matmul(b[:], wa2[:, pair * P:(pair + 1) * P], gaT[0:GLA_RANK, :],
                                             start=True, stop=True).then_inc(bank_full, 1)
                    elif kind == "VT":
                        b = open_bank(l, word)
                        pe.wait_ge(gv_ready, l * 4 + i + 1)
                        for t in range(TT):
                            last = nc.tensor.transpose(b[:, t * P:(t + 1) * P], vtmp[:, i % 2, t * P:(t + 1) * P], ident)
                        last.then_inc(bank_full, 1)
                    elif kind == "KT":
                        b = open_bank(l, word)
                        pe.wait_ge(gla_qk, l * 2 + i + 1)
                        for t in range(TT):
                            last = nc.tensor.transpose(b[:, t * P:(t + 1) * P], gk[:, i, t * P:(t + 1) * P], ident)
                        last.then_inc(bank_full, 1)
                    elif kind == "ATT":
                        b = open_bank(l, word)
                        pe.wait_ge(gla_qk, l * 2 + i // 2 + 1)
                        r = GLA_DK * (i % 2)
                        for t in range(TT):
                            s = slice(t * P, (t + 1) * P)
                            last = nc.tensor.matmul(b[:, s], kin[r:r + GLA_DK, i // 2, s], gq[r:r + GLA_DK, i // 2, s],
                                                    start=True, stop=True)
                        last.then_inc(bank_full, 1)
                    elif kind == "KV":
                        pe.wait_ge(kendT_ready, l * 2 + i + 1)
                        pe.wait_ge(vT_ready, l * 4 + 2 * i + 2)
                        for odd in range(2):
                            b = open_bank(l, word + "ab"[odd], True)
                            r = GLA_CHUNK * odd
                            for h in range(2):
                                for t in range(TT):
                                    last = nc.tensor.matmul(
                                        b[GLA_DK * h:GLA_DK * (h + 1), t * P:(t + 1) * P],
                                        kendT[r:r + GLA_CHUNK, i, t, GLA_DK * h:GLA_DK * (h + 1)],
                                        vT[r:r + GLA_CHUNK, 2 * i + h, t, :], start=True, stop=True)
                            last.then_inc(bank_full, 1)
                    elif kind == "GO":
                        b = open_bank(l, word)
                        pe.wait_ge(att_ready, l * 4 + i + 1)
                        pe.wait_ge(vT_ready, l * 4 + i + 1)
                        pe.wait_ge(states_ready, l * 2 + i // 2 + 1)
                        r = GLA_DK * (i % 2)
                        for t in range(TT):
                            nc.tensor.matmul(b[:, t * P:(t + 1) * P], vT[:, i, t, :], attm[:, i % 2, t, :],
                                             start=True, stop=False)
                            for c in (2 * t, 2 * t + 1):
                                if c:
                                    s = slice(c * GLA_CHUNK, (c + 1) * GLA_CHUNK)
                                    last = nc.tensor.matmul(b[:, s], S[r:r + GLA_DK, i // 2, c - 1, :],
                                                            gq[r:r + GLA_DK, i // 2, s], start=False,
                                                            stop=c == 2 * t + 1)
                        last.then_inc(bank_full, 1)
                    elif kind == "QSUM":
                        b = open_bank(l, word)
                        pe.wait_ge(swa_sq, l * 5 + 5)
                        for i in range(5):
                            source = sqk[:] if i == 4 else sqr[:, i, :]
                            for t in range(TT):
                                last = nc.tensor.matmul(b[:, HEADS_Q * t + 2 * i:HEADS_Q * t + 2 * i + 2],
                                                        source[:, t * P:(t + 1) * P], blk, start=True, stop=True)
                        last.then_inc(bank_full, 1)
                    elif kind == "OSUM":
                        b = open_bank(l, word)
                        pe.wait_ge(yo_sq, l * 4 + 4)
                        for h in range(GLA_HEADS):
                            for t in range(TT):
                                last = nc.tensor.matmul(b[:, GLA_HEADS * t + h:GLA_HEADS * t + h + 1],
                                                        sqo[:, h, t * P:(t + 1) * P], ones, start=True, stop=True)
                        last.then_inc(bank_full, 1)
                    elif kind == "QN":
                        rows(l, word, 2, 1, lambda t: [HEADS_Q * t + 2 * i, HEADS_Q * t + 2 * i + 1])
                    elif kind == "ON":
                        rows(l, word, 3, 3, lambda t: [GLA_HEADS * t + i])
                    elif kind == "VS":
                        b = open_bank(l, word)
                        pe.wait_ge(sv_ready, l + 1)
                        for t in range(TT):
                            last = nc.tensor.transpose(b[:, t * P:(t + 1) * P], vtmp[:, 0, t * P:(t + 1) * P], ident)
                        last.then_inc(bank_full, 1)
                    elif kind == "SC":
                        kv, n = i // TT, i % TT
                        pe.wait_ge(swa_roped, l * 5 + 3 + 2 * kv)
                        for odd in range(2):
                            b = open_bank(l, word + "ab"[odd])
                            r = SWA_DIM * odd
                            first = 0 if n else P
                            for j in range(2):
                                last = nc.tensor.matmul(
                                    b[:, j * 2 * P + first:(j + 1) * 2 * P],
                                    sq[r:r + SWA_DIM, 2 * kv + j, n * P:(n + 1) * P],
                                    kd[r:r + SWA_DIM, kv, (n - 1) * P + first:(n + 1) * P], start=True, stop=True)
                            last.then_inc(bank_full, 1)
                    elif kind == "PT":
                        pe.wait_ge(probs_ready, l * 8 + i + 1)
                        for cur in ((0, 1) if i % TT else (1,)):
                            b = open_bank(l, word + ("cur" if cur else "prev"))
                            for h in range(4):
                                last = nc.tensor.transpose(b[:, h * P:(h + 1) * P], sm[i % 2][:, h, cur * P:(cur + 1) * P], ident)
                            last.then_inc(bank_full, 1)
                    elif kind == "PV":
                        kv, n = i // TT, i % TT
                        b = open_bank(l, word)
                        pe.wait_ge(vs_ready, l + 1)
                        if n:
                            pe.wait_ge(pprev_ready, l * 6 + kv * 3 + n)
                            nc.tensor.matmul(b[:], vd[:, kv, n - 1].rearrange("p a d -> p (a d)"),
                                             pT[:, 0].rearrange("p h c -> p (h c)"), start=True, stop=False)
                        pe.wait_ge(pcur_ready, l * 8 + i + 1)
                        nc.tensor.matmul(b[:], vd[:, kv, n].rearrange("p a d -> p (a d)"),
                                         pT[:, 1].rearrange("p h c -> p (h c)"), start=n == 0,
                                         stop=True).then_inc(bank_full, 1)
                with pe.Fori(0, N_BRANCH) as g:
                    for pos in range(GATE_IT):
                        if pos % 8 < 4:
                            unit(l, G0, g, pos, u_tile(uh), u_tile(ul))
                        else:
                            def branches_ready():
                                pe.wait_ge(yconv_ready, l * 4 + 4)
                                pe.wait_ge(ygla_ready, l * 4 + 4)
                                pe.wait_ge(yswa_ready, l * 8 + 8)

                            def y_tile(t):
                                return lambda k: t[:, bass.ds(g * BK + k, 1), :].rearrange("p a n -> p (a n)")
                            unit(l, G0, g, pos, y_tile(yh), y_tile(yl), gate=branches_ready if pos == 4 else None)
                for pos in range(KT):
                    if pos == 0:
                        unit(l, O0, 0, pos, u_tile(yh), u_tile(yl), mx_ready, lambda k: l * 8 + k + 1)
                    else:
                        unit(l, O0, 0, pos, u_tile(yh), u_tile(yl))

                def mlp_quarter(q, first):
                    for pos in range(MLP_IT):
                        if pos == 0 and first:
                            unit(l, M0, q, pos, u_tile(uh), u_tile(ul), u_ready, lambda k: l * 16 + 8 + k + 1)
                            sum_squares(l, "NSUM2", 8)
                        elif pos < 8:
                            unit(l, M0, q, pos, u_tile(uh), u_tile(ul))
                            if pos == 2 and first:
                                rows(l, "NROW2", 4, 1, lambda t: [t])
                        elif pos == 8:
                            unit(l, M0, q, pos, u_tile(yh), u_tile(yl), hid_ready,
                                 lambda k: l * 32 + q * 8 + (k + 1 + HID_CREDIT))
                        else:
                            unit(l, M0, q, pos, u_tile(yh), u_tile(yl))

                mlp_quarter(0, True)
                with pe.Fori(1, QUARTERS) as q:
                    mlp_quarter(q, False)
            pe.wait_ge(x_upd, 8 + 16 * DEPTH)
            for e in range(2 * TT):
                t, half = e // 2, e % 2
                pe.wait_ge(bank_free[e % 4], DEPTH * bank_fills(e % 4) + XF // 4 + e // 4 + 1)
                for j in range(4):
                    last = nc.tensor.transpose(bank[e % 4][:, j * P:(j + 1) * P], xT[:, 4 * half + j, t * P:(t + 1) * P], ident)
                last.then_inc(bank_full, 1)

        @block.scalar
        def _(act):
            act.dma_start(pos_i[:], positions.partition_broadcast(P)).then_inc(pos_full, 16)
            act.dma_start(nw[:], norms).then_inc(nw_full, 16)
            act.dma_start(gm[:], gmask).then_inc(gm_full, 16)

            def filled(l, name):
                f = FILL[name]
                act.wait_ge(bank_full, l * N_FILLS + XF + f + 1)
                return bank[f % 4], bank_free[f % 4]

            def split_high(l, base, it, pos):
                act.wait_ge(raw_full[slab_slot(base, pos)], (l * HALF_SLABS + slab_half(base, it, pos)) * 16 + 16)
                act.wait_ge(unit_done, l * UNITS + unit_index(base, it, pos) + 1)
                nc.scalar.activation(split_view(wh, base, pos), raw_view(base, pos), ACT.Copy).then_inc(
                    hi_done, 2 if base == 0 and pos == 0 else 1)

            def done(l, base, it, pos):
                act.wait_ge(unit_done, l * UNITS + unit_index(base, it, pos) + 1 + UNIT_CREDIT)
                return acc[(base + pos) % 4], acc_free[(base + pos) % 4]

            def norm_tile(e, k, weight, wait_temp=True):
                act.wait_ge(x_upd, e + 1)
                nc.scalar.activation(uh[:, k, :], xT[:, k, :], ACT.Copy, scale=weight).then_inc(u_hi, 1)
                if wait_temp:
                    act.wait_ge(x_acc, e - 1)
                nc.scalar.activation(T[k % 2], xT[:, k, :], ACT.Square).then_inc(x_sq, 1)

            act.wait_ge(ready0, 1)
            act.wait_ge(angle_ready, 1)
            nc.scalar.activation(sinT[:], sq[:, 1, :], ACT.Sin)
            nc.scalar.activation(sq[:, 3, :], sq[:, 1, :], ACT.Sin, scale=0.5).then_inc(sines_ready, 1)
            act.wait_ge(nw_full, 16)
            for k in range(KT):
                norm_tile(k, k, nw[:, k:k + 1], k >= 2)

            with act.Fori(0, DEPTH) as l:
                for pos in (0, 2):
                    split_high(l, 0, 0, pos)
                for word in SEQUENCE:
                    kind, i = step_of(word)
                    nc.scalar.drain()
                    if word in UNIT:
                        pos = UNIT[word]
                        split_high(l, *ahead(0, 0, pos))
                        if kind == "ga":
                            split_high(l, *ahead(0, 0, pos + 1))
                        if kind in ("sq", "sk"):
                            act.wait_ge(swa_raw, l * 5 + (4 if kind == "sk" else i) + 1)
                            nc.scalar.activation(sqk[:] if kind == "sk" else sqr[:, i, :],
                                                 ct[:] if kind == "sk" else sq[:, i, :], ACT.Square).then_inc(swa_sq, 1)
                        elif kind == "cb":
                            act.wait_ge(y_val, l * 8 + i + 1)
                            nc.scalar.activation(yh[:, i, :], T[0], ACT.Copy).then_inc(y_hi, 1)
                        elif kind == "gr":
                            act.wait_ge(gr_scaled, l * 4 + i + 1)
                            nc.scalar.activation(ct[:], T[i % 2], ACT.Tanh, scale=0.5).then_inc(gr_tanh, 1)
                            act.wait_ge(y_val, l * 8 + 4 + i + 1)
                            nc.scalar.activation(yh[:, 4 + i, :], T[i % 2], ACT.Copy).then_inc(y_hi, 1)
                    elif kind == "ZA":
                        act.wait_ge(z_biased, l * 2 + 2)
                        nc.scalar.activation(eb[:], gb[:], ACT.Abs)
                        nc.scalar.drain()
                        nc.scalar.activation(eb[:], eb[:], ACT.Exp, scale=-1.0)
                        nc.scalar.drain()
                        nc.scalar.activation(eb[:], eb[:], ACT.Ln, bias=one_col).then_inc(softplus_ready, 1)
                    elif kind == "ZB":
                        act.wait_ge(b_ready, l + 1)
                        nc.scalar.activation(eb[:], gb[:], ACT.Exp, scale=1.0 / 16)
                        nc.scalar.activation(kin[:], gb[:], ACT.Exp, scale=-1.0 / 16)
                        nc.scalar.drain()
                        nc.scalar.activation(gb[:], T3[:, 0:2, :], ACT.Exp, scale=-1.0 / 16).then_inc(gla_exps, 1)
                    elif kind == "VT":
                        b, free = filled(l, word)
                        nc.scalar.activation(vT[:, i].rearrange("p t n -> p (t n)"), b[:], ACT.Copy).then_inc(free, 1)
                        nc.scalar.drain().then_inc(vT_ready, 1)
                    elif kind == "KT":
                        b, free = filled(l, word)
                        nc.scalar.activation(kendT[:, i].rearrange("p t n -> p (t n)"), b[:], ACT.Copy).then_inc(free, 1)
                        nc.scalar.drain().then_inc(kendT_ready, 1)
                    elif kind == "GO":
                        b, free = filled(l, word)
                        nc.scalar.activation(yo[:, i, :], b[:], ACT.Copy).then_inc(free, 1)
                        nc.scalar.drain().then_inc(yo_ready, 1)
                        nc.scalar.activation(sqo[:, i, :], yo[:, i, :], ACT.Square).then_inc(yo_sq, 1)
                    elif kind == "SC":
                        act.wait_ge(scores_ready, l * 8 + i + 1)
                        keys = slice(0, 2 * P) if i % TT else slice(P, 2 * P)
                        buf = i % 2
                        for h in range(4):
                            nc.scalar.activation(sm[buf][:, h, keys], sm[buf][:, h, keys], ACT.Exp,
                                                 bias=neg4[buf][:, h:h + 1], accum_out=sum4[buf][:, h:h + 1])
                        nc.scalar.activation(es4[buf], d4[buf], ACT.Exp).then_inc(exps_ready, 1)
                    elif kind == "SM":
                        act.wait_ge(den_ready, l * 8 + i + 1)
                        keys = slice(0, 2 * P) if i % TT else slice(P, 2 * P)
                        for h in range(4):
                            last = nc.scalar.activation(sm[i % 2][:, h, keys], sm[i % 2][:, h, keys], ACT.Copy,
                                                        scale=den4[i % 2][:, h:h + 1])
                        last.then_inc(probs_ready, 1)
                    elif kind == "PT":
                        for cur in ((0, 1) if i % TT else (1,)):
                            b, free = filled(l, word + ("cur" if cur else "prev"))
                            nc.scalar.activation(pT[:, cur].rearrange("p h c -> p (h c)"), b[:], ACT.Copy).then_inc(free, 1)
                            nc.scalar.drain().then_inc(pcur_ready if cur else pprev_ready, 1)
                    elif kind == "PV":
                        b, _ = filled(l, word)
                        kv, n = i // TT, i % TT
                        for odd in range(2):
                            r = slice(SWA_DIM * odd, SWA_DIM * (odd + 1))
                            last = nc.scalar.activation(
                                yh[r, 8 + 2 * kv:10 + 2 * kv, n * P:(n + 1) * P],
                                b[r, 2 * odd * P:(2 * odd + 2) * P].rearrange("p (j c) -> p j c", j=2), ACT.Copy)
                        last.then_inc(pv_hi, 1)

                def gates(g, final):
                    for pos in range(GATE_IT):
                        split_high(l, *ahead(G0, g, pos))
                        if pos % 8 < 4:
                            act.wait_ge(gate_scaled, l * 24 + g * 8 + (pos // 8 * 4 + pos % 4 + 1))
                            nc.scalar.activation(gt[:, pos % 4, :], gt[:, pos % 4, :], ACT.Tanh, scale=0.5).then_inc(gate_ready, 1)
                        elif final:
                            d = pos // 8 * 4 + pos % 4
                            act.wait_ge(mixed_done, l * 8 + d + 1)
                            nc.scalar.activation(yh[:, d, :], mixed[:, d, :], ACT.Copy, scale=0.5).then_inc(mx_hi, 1)

                with act.Fori(0, N_BRANCH - 1) as g:
                    gates(g, False)
                gates(N_BRANCH - 1, True)
                for pos in range(KT):
                    split_high(l, *ahead(O0, 0, pos))
                    norm_tile(l * 16 + (8 + pos), pos, nw[:, bass.ds(l * KT + (DEPTH * KT + pos), 1)])

                def mlp_quarter(q, final):
                    for pos in range(MLP_IT):
                        if not (final and pos + AHEAD >= MLP_IT):
                            split_high(l, *ahead(M0, q, pos))
                        if pos < 8:
                            a, free = done(l, M0, q, pos)
                            act.wait_ge(hid_ready, l * 32 + q * 8 + (pos - 1 + HID_CREDIT))
                            nc.scalar.activation(T[pos % 2], a[:], ACT.Relu).then_inc(free, 1)
                            nc.scalar.drain().then_inc(relu_ready, 1)
                            act.wait_ge(hid_val, l * 32 + q * 8 + (pos + 1))
                            nc.scalar.activation(yh[:, pos, :], T[pos % 2], ACT.Copy).then_inc(hid_hi, 1)
                        elif final:
                            k = pos - 8
                            norm_tile(l * 16 + (16 + k), k, nw[:, bass.ds(l * KT + (KT + k), 1)])

                with act.Fori(0, QUARTERS - 1) as q:
                    mlp_quarter(q, False)
                mlp_quarter(QUARTERS - 1, True)

        @block.vector
        def _(dve):
            V = nc.vector
            for s, n in ([(x, 1) for x in raw_free + acc_free + bank_free + [par_free]]
                         + [(hid_ready, HID_CREDIT)]):
                dve.sem_inc(s, n)
            V.memset(one_col, 1.0)
            V.drain().then_inc(ready0, 1)

            def filled(l, name, plain=False):
                f = FILL[name]
                fills = dve.to_reg(l * N_FILLS + (XF + f + 1))
                if plain:
                    dve.wait_ge(in_full, 16)
                dve.wait_ge(bank_full, fills)
                return bank[f % 4], bank_free[f % 4]

            def split_low(l, base, it, pos):
                dve.wait_ge(hi_done, l * UNITS + unit_index(base, it, pos) + (2 if base == 0 and pos == 0 else 1))
                V.tensor_tensor(split_view(wl, base, pos), raw_view(base, pos), split_view(wh, base, pos).bitcast(f32),
                                ALU.subtract).then_inc(lo_done, 2 if base == 0 and pos == 0 else 1)
                if slab_ends(base, pos) or (base == 0 and pos == 0):
                    V.drain().then_inc(raw_free[slab_slot(base, pos)], 1)

            def done(l, base, it, pos):
                dve.wait_ge(unit_done, l * UNITS + unit_index(base, it, pos) + 1 + UNIT_CREDIT)
                return acc[(base + pos) % 4], acc_free[(base + pos) % 4]

            def norm_tile(e, k, weight):
                dve.wait_ge(u_hi, e + 1)
                V.scalar_tensor_tensor(out=ul[:, k, :], in0=xT[:, k, :], scalar=weight, in1=uh[:, k, :].bitcast(f32),
                                       op0=ALU.mult, op1=ALU.subtract).then_inc(u_ready, 1)
                dve.wait_ge(x_sq, e + 1)
                if k == 0:
                    V.tensor_copy(nacc[:], T[0]).then_inc(x_acc, 1)
                else:
                    V.tensor_tensor(nacc[:], nacc[:], T[k % 2], ALU.add).then_inc(x_acc, 1)

            def scaled_q(l, i):
                a, free = done(l, 0, 0, UNIT[f"gq{i}"])
                V.scalar_tensor_tensor(out=gq[:, i, :], in0=a[:], scalar=GLA_DK ** -0.5, in1=rs[:],
                                       op0=ALU.mult, op1=ALU.mult).then_inc(free, 1)

            def rsqrt(l, name, columns, n, result, square=False):
                b, free = filled(l, name)
                a, y, t = (stat[:, j, 0:columns] for j in (0, result, 2))
                bits = stat_i[:, 0:columns]
                V.tensor_scalar(a, b[:, 0:columns], 1.0 / n, EPS, ALU.mult, ALU.add).then_inc(free, 1)
                V.drain()
                V.tensor_scalar(bits, a.bitcast(i32), 1, None, ALU.logical_shift_right)
                V.drain()
                V.tensor_scalar(y.bitcast(i32), bits, -1, 0x5F3759DF, ALU.mult, ALU.add)
                V.drain()
                for _ in range(3):
                    V.tensor_tensor(t, a, y, ALU.mult)
                    V.drain()
                    V.scalar_tensor_tensor(out=t, in0=t, scalar=-0.5, in1=y, op0=ALU.mult, op1=ALU.mult)
                    V.drain()
                    V.scalar_tensor_tensor(out=y, in0=t, scalar=1.5, in1=y, op0=ALU.add, op1=ALU.mult)
                    V.drain()
                if square:
                    V.tensor_tensor(y, y, y, ALU.mult)
                    V.drain()
                V.drain().then_inc(stat_ready, 1)

            dve.wait_ge(in_full, 16)
            dve.wait_ge(pos_full, 16)
            V.tensor_copy(sq[:, 2, :], pos_i[:])
            V.drain()
            V.tensor_scalar(sq[:, 1, :], sq[:, 2, :], invf, None, ALU.mult)
            V.drain()
            V.tensor_scalar(sq[:, 2, :], sq[:, 1, :], 1.0 / TWO_PI, ROUND, ALU.mult, ALU.add)
            V.drain()
            V.tensor_scalar(sq[:, 3, :], sq[:, 2, :], -ROUND, None, ALU.add)
            V.drain()
            for part in (PI_1, PI_2, PI_3):
                V.scalar_tensor_tensor(out=sq[:, 1, :], in0=sq[:, 3, :], scalar=-part, in1=sq[:, 1, :],
                                       op0=ALU.mult, op1=ALU.add)
                V.drain()
            V.tensor_scalar(sq[:, 1, :], sq[:, 1, :], 3.1415925, -3.1415925, ALU.min, ALU.max).then_inc(angle_ready, 1)
            dve.wait_ge(sines_ready, 1)
            V.tensor_tensor(cosT[:], sq[:, 3, :], sq[:, 3, :], ALU.mult)
            V.tensor_scalar(sinT[:], sinT[:], sign, None, ALU.mult)
            V.drain()
            V.tensor_scalar(cosT[:], cosT[:], -2.0, 1.0, ALU.mult, ALU.add)
            dve.wait_ge(nw_full, 16)
            for k in range(KT + 1):
                V.drain()
                if k < KT:
                    dve.wait_ge(bank_full, k + 1)
                    V.tensor_copy(xT[:, k, :], bank[k % 4][:]).then_inc(bank_free[k % 4], 1)
                    V.drain().then_inc(x_upd, 1)
                if k:
                    norm_tile(k - 1, k - 1, nw[:, k - 1:k])
            dve.wait_ge(gm_full, 16)

            with dve.Fori(0, DEPTH) as l:
                for pos in (0, 2):
                    split_low(l, 0, 0, pos)
                dve.wait_ge(par_full, l * 32 + 32)
                V.tensor_scalar(qn8, par[:, PC["qn"]:PC["qn"] + 1], SWA_DIM ** -0.5, None, ALU.mult)
                V.memset(attm[:], 0.0)
                for word in SEQUENCE:
                    kind, i = step_of(word)
                    V.drain()
                    if word in UNIT:
                        pos = UNIT[word]
                        if kind != "ga":
                            split_low(l, *ahead(0, 0, pos))
                        if kind == "ga":
                            split_low(l, *ahead(0, 0, pos))
                            V.drain().then_inc(acc_free[1], 1)
                            split_low(l, *ahead(0, 0, pos + 1))
                        elif kind == "gq" and i:
                            scaled_q(l, i)
                        elif kind == "gk":
                            a, free = done(l, 0, 0, pos)
                            V.tensor_tensor(gk[:, i, :], a[:], rs[:], ALU.mult).then_inc(free, 1)
                        elif kind == "gv":
                            if i >= 2:
                                dve.wait_ge(bank_full, l * N_FILLS + XF + FILL[f"VT{i - 2}"] + 1)
                            a, free = done(l, 0, 0, pos)
                            V.tensor_tensor(vtmp[:, i % 2, :], a[:], rs[:], ALU.mult).then_inc(free, 1)
                            V.drain().then_inc(gv_ready, 1)
                        elif kind == "sv":
                            dve.wait_ge(bank_full, l * N_FILLS + XF + FILL["VT2"] + 1)
                            a, free = done(l, 0, 0, pos)
                            V.tensor_tensor(vtmp[:, 0, :], a[:], rs[:], ALU.mult).then_inc(free, 1)
                            V.drain().then_inc(sv_ready, 1)
                        elif kind in ("sq", "sk"):
                            a, free = done(l, 0, 0, pos)
                            V.tensor_tensor(ct[:] if kind == "sk" else sq[:, i, :], a[:], rs[:], ALU.mult).then_inc(free, 1)
                            V.drain().then_inc(swa_raw, 1)
                        elif kind == "cx":
                            a, free = done(l, 0, 0, pos)
                            V.tensor_tensor(cu[:, i, :], a[:], rs_sq, ALU.mult).then_inc(free, 1)
                        elif kind == "cc":
                            a, free = done(l, 0, 0, pos)
                            V.tensor_tensor(cu[:, i, :], a[:], cu[:, i, :], ALU.mult).then_inc(free, 1)
                        elif kind == "cb":
                            w = [par[:, PC["cw"] + 4 * k + i:PC["cw"] + 4 * k + i + 1] for k in range(3)]
                            V.tensor_scalar(ct[:], cu[:, i, :], w[2], par[:, PC["cb"] + i:PC["cb"] + i + 1], ALU.mult, ALU.add)
                            V.drain()
                            for back in (1, 2):
                                V.scalar_tensor_tensor(out=ct[:, back:], in0=cu[:, i, 0:SEQ - back], scalar=w[2 - back],
                                                       in1=ct[:, back:], op0=ALU.mult, op1=ALU.add)
                                V.drain()
                            V.tensor_tensor(ct[:], ct[:], rs[:], ALU.mult)
                            V.drain()
                            a, free = done(l, 0, 0, pos)
                            V.tensor_tensor(T[0], a[:], ct[:], ALU.mult).then_inc(free, 1)
                            V.drain().then_inc(y_val, 1)
                            dve.wait_ge(y_hi, l * 8 + i + 1)
                            V.tensor_tensor(yl[:, i, :], T[0], yh[:, i, :].bitcast(f32), ALU.subtract).then_inc(yconv_ready, 1)
                        elif kind == "gr":
                            t = T[i % 2]
                            a, free = done(l, 0, 0, pos)
                            V.tensor_tensor(t, a[:], rs[:], ALU.mult).then_inc(free, 1)
                            V.drain().then_inc(gr_scaled, 1)
                            dve.wait_ge(gr_tanh, l * 4 + i + 1)
                            V.scalar_tensor_tensor(out=t, in0=ct[:], scalar=1.0, in1=t, op0=ALU.add, op1=ALU.mult)
                            V.drain()
                            V.scalar_tensor_tensor(out=t, in0=t, scalar=0.5, in1=yo[:, i, :], op0=ALU.mult, op1=ALU.mult)
                            V.drain().then_inc(y_val, 1)
                            dve.wait_ge(y_hi, l * 8 + 4 + i + 1)
                            V.tensor_tensor(yl[:, 4 + i, :], t, yh[:, 4 + i, :].bitcast(f32), ALU.subtract).then_inc(ygla_ready, 1)
                    elif kind == "NSUM":
                        rsqrt(l, word, TT, D_MODEL, 1)
                    elif kind == "NROW":
                        b, free = filled(l, word)
                        V.tensor_copy(rs[:], b[:]).then_inc(free, 1)
                        V.drain()
                        a, free = done(l, 0, 0, UNIT["ga"])
                        V.tensor_tensor(gaT[0:GLA_RANK, :], a[0:GLA_RANK, :], rs[0:GLA_RANK, :], ALU.mult).then_inc(free, 1)
                        V.drain().then_inc(ga_ready, 1)
                        scaled_q(l, 0)
                        V.tensor_tensor(rs_sq, rs[:], rs[:], ALU.mult)
                    elif kind == "ZA":
                        for pair in range(2):
                            b, free = filled(l, word + "ab"[pair])
                            V.tensor_scalar(gb[:, pair, :], b[:], par[:, PC["ba"] + pair:PC["ba"] + pair + 1], None,
                                            ALU.add).then_inc(free, 1)
                            V.drain().then_inc(z_biased, 1)
                    elif kind == "ZB":
                        dve.wait_ge(softplus_ready, l + 1)
                        V.scalar_tensor_tensor(out=kin[:], in0=gb[:], scalar=0.0, in1=eb[:], op0=ALU.min, op1=ALU.subtract)
                        V.drain()
                        for pair in range(2):
                            V.tensor_tensor_scan(gb[:, pair, :], scanm, kin[:, pair, :], 0.0, ALU.mult, ALU.add)
                        V.drain()
                        bc = gb[:].rearrange("p h (c n) -> p (h c) n", n=GLA_CHUNK)
                        V.tensor_tensor(T3[:, 0:2, :].rearrange("p h (c n) -> p (h c) n", n=GLA_CHUNK), bc,
                                        bc[:, :, GLA_CHUNK - 1:GLA_CHUNK].broadcast_to([P, 2 * CHUNKS, GLA_CHUNK]),
                                        ALU.subtract).then_inc(b_ready, 1)
                    elif kind == "X":
                        dve.wait_ge(gla_exps, l + 1)
                        V.tensor_tensor(gq[:, i, :], gq[:, i, :], eb[:, i, :], ALU.mult)
                        V.tensor_tensor(kin[:, i, :], gk[:, i, :], kin[:, i, :], ALU.mult)
                        V.drain()
                        V.tensor_tensor(gk[:, i, :], gk[:, i, :], gb[:, i, :], ALU.mult).then_inc(gla_qk, 1)
                    elif kind == "ATT":
                        if i >= 2:
                            dve.wait_ge(bank_full, l * N_FILLS + XF + FILL[f"GO{i - 2}"] + 1)
                        b, free = filled(l, word, True)
                        for t in range(TT):
                            last = V.copy_predicated(attm[:, i % 2, t, :], gm[:], b[:, t * P:(t + 1) * P])
                        last.then_inc(free, 1)
                        V.drain().then_inc(att_ready, 1)
                    elif kind == "KV":
                        be, free_e = filled(l, word + "a")
                        bo, free_o = filled(l, word + "b")
                        V.tensor_copy(S[:, i, 0, :], be[:, 0:P])
                        for c in range(1, CHUNKS - 1):
                            V.drain()
                            b = (be, bo)[c % 2]
                            last_c = GLA_CHUNK * (c + 1) - 1
                            V.scalar_tensor_tensor(out=S[:, i, c, :], in0=S[:, i, c - 1, :], scalar=eb[:, i, last_c:last_c + 1],
                                                   in1=b[:, c // 2 * P:(c // 2 + 1) * P], op0=ALU.mult, op1=ALU.add)
                        V.drain().then_inc(free_e, 1)
                        V.drain().then_inc(free_o, 1)
                        V.drain().then_inc(states_ready, 1)
                    elif kind == "QSUM":
                        rsqrt(l, word, TT * HEADS_Q, SWA_DIM, 1)
                    elif kind == "OSUM":
                        rsqrt(l, word, TT * GLA_HEADS, GLA_DV, 3)
                    elif kind == "QN":
                        t = ct[:] if i == 4 else sq[:, i, :]
                        w = par[:, PC["kn"]:PC["kn"] + 1] if i == 4 else qn8
                        b, free = filled(l, word)
                        V.scalar_tensor_tensor(out=t, in0=t, scalar=w, in1=b[:], op0=ALU.mult, op1=ALU.mult).then_inc(free, 1)
                        V.drain()
                        V.stream_shuffle(T[0], t, ROPE_SWAP)
                        V.drain()
                        V.tensor_tensor(T[0], T[0], sinT[:], ALU.mult)
                        V.tensor_tensor(t, t, cosT[:], ALU.mult)
                        V.drain()
                        if i < 4:
                            V.tensor_tensor(t, t, T[0], ALU.add).then_inc(swa_roped, 1)
                        else:
                            for kv in range(2):
                                src = slice(SWA_DIM * kv, SWA_DIM * (kv + 1))
                                for half in range(2):
                                    V.tensor_tensor(kd[SWA_DIM * half:SWA_DIM * (half + 1), kv, :], ct[src, :],
                                                    T[0][src, :], ALU.add)
                            V.drain().then_inc(swa_roped, 1)
                    elif kind == "ON":
                        dve.wait_ge(yo_ready, l * 4 + i + 1)
                        b, free = filled(l, word)
                        V.scalar_tensor_tensor(out=yo[:, i, :], in0=yo[:, i, :], scalar=par[:, PC["on"]:PC["on"] + 1],
                                               in1=b[:], op0=ALU.mult, op1=ALU.mult).then_inc(free, 1)
                    elif kind == "VS":
                        b, free = filled(l, word)
                        bv = b[:].rearrange("p (t k d) -> p t k d", t=TT, k=2)
                        for kv in range(2):
                            for half in range(2):
                                last = V.tensor_copy(vd[:, kv, :, half, :], bv[:, :, kv, :])
                        last.then_inc(free, 1)
                        V.drain().then_inc(vs_ready, 1)
                    elif kind == "SC":
                        first, buf = 0 if i % TT else P, i % 2
                        if i >= 2:
                            dve.wait_ge(bank_full, l * N_FILLS + XF + FILL[f"PT{i - 2}cur"] + 1)
                        for odd in range(2):
                            b, free = filled(l, word + "ab"[odd])
                            V.tensor_tensor(sm[buf][:, 2 * odd:2 * odd + 2, first:],
                                            b[:].rearrange("p (j c) -> p j c", j=2)[:, :, first:],
                                            swam.unsqueeze(1).broadcast_to([P, 2, 2 * P])[:, :, first:], ALU.add).then_inc(free, 1)
                        V.drain()
                        V.tensor_reduce(m4, sm[buf][:, :, first:], AX.X, ALU.max)
                        V.drain()
                        sink = par[:, PC["sink"] + i // TT * 4:PC["sink"] + i // TT * 4 + 4]
                        V.tensor_tensor(m4, m4, sink, ALU.max)
                        V.drain()
                        V.tensor_scalar(neg4[buf], m4, -1.0, None, ALU.mult)
                        V.tensor_tensor(d4[buf], sink, m4, ALU.subtract)
                        V.drain().then_inc(scores_ready, 1)
                    elif kind == "SM":
                        dve.wait_ge(exps_ready, l * 8 + i + 1)
                        V.tensor_tensor(den4[i % 2], sum4[i % 2], es4[i % 2], ALU.add)
                        V.drain()
                        V.reciprocal(den4[i % 2], den4[i % 2])
                        V.drain().then_inc(den_ready, 1)
                    elif kind == "PV":
                        b, free = filled(l, word)
                        kv, n = i // TT, i % TT
                        dve.wait_ge(pv_hi, l * 8 + i + 1)
                        for odd in range(2):
                            r = slice(SWA_DIM * odd, SWA_DIM * (odd + 1))
                            at_y = (r, slice(8 + 2 * kv, 10 + 2 * kv), slice(n * P, (n + 1) * P))
                            last = V.tensor_tensor(yl[at_y], b[r, 2 * odd * P:(2 * odd + 2) * P].rearrange("p (j c) -> p j c", j=2),
                                                   yh[at_y].bitcast(f32), ALU.subtract)
                        last.then_inc(free, 1)
                        V.drain().then_inc(yswa_ready, 1)
                V.drain().then_inc(par_free, 1)
                V.memset(mixed[:], 0.0)

                def mixed_low(d):
                    dve.wait_ge(mx_hi, l * 8 + d + 1)
                    V.scalar_tensor_tensor(out=yl[:, d, :], in0=mixed[:, d, :], scalar=0.5, in1=yh[:, d, :].bitcast(f32),
                                           op0=ALU.mult, op1=ALU.subtract).then_inc(mx_ready, 1)

                def gates(g, final):
                    for pos in range(GATE_IT):
                        d = pos // 8 * 4 + pos % 4
                        V.drain()
                        split_low(l, *ahead(G0, g, pos))
                        if pos % 8 < 4:
                            if final and pos == 8:
                                mixed_low(d - 1)
                            a, free = done(l, G0, g, pos)
                            V.tensor_tensor(gt[:, pos % 4, :], a[:], rs[:], ALU.mult).then_inc(free, 1)
                            V.drain().then_inc(gate_scaled, 1)
                        else:
                            dve.wait_ge(gate_ready, l * 24 + g * 8 + (d + 1))
                            if final and pos % 4:
                                mixed_low(d - 1)
                            a, free = done(l, G0, g, pos)
                            V.scalar_tensor_tensor(out=T[pos % 2], in0=gt[:, pos % 4, :], scalar=1.0, in1=a[:],
                                                   op0=ALU.add, op1=ALU.mult).then_inc(free, 1)
                            V.drain()
                            V.tensor_tensor(mixed[:, d, :], mixed[:, d, :], T[pos % 2], ALU.add)
                            if final:
                                V.drain().then_inc(mixed_done, 1)

                with dve.Fori(0, N_BRANCH - 1) as g:
                    gates(g, False)
                gates(N_BRANCH - 1, True)
                mixed_low(KT - 1)
                for pos in range(KT):
                    V.drain()
                    split_low(l, *ahead(O0, 0, pos))
                    a, free = done(l, O0, 0, pos)
                    V.tensor_tensor(xT[:, pos, :], xT[:, pos, :], a[:], ALU.add).then_inc(free, 1)
                    V.drain().then_inc(x_upd, 1)
                    norm_tile(l * 16 + (8 + pos), pos, nw[:, bass.ds(l * KT + (DEPTH * KT + pos), 1)])

                def mlp_quarter(q, first=False, final=False):
                    for pos in range(MLP_IT):
                        V.drain()
                        if not (final and pos + AHEAD >= MLP_IT):
                            split_low(l, *ahead(M0, q, pos))
                        if pos < 8:
                            t = T[pos % 2]
                            dve.wait_ge(relu_ready, l * 32 + q * 8 + (pos + 1))
                            V.tensor_tensor(t, t, t, ALU.mult).then_inc(hid_val, 1)
                            dve.wait_ge(hid_hi, l * 32 + q * 8 + (pos + 1))
                            V.tensor_tensor(yl[:, pos, :], t, yh[:, pos, :].bitcast(f32), ALU.subtract).then_inc(hid_ready, 1)
                            if first and pos == 0:
                                rsqrt(l, "NSUM2", TT, D_MODEL, 1, square=True)
                            elif first and pos == 2:
                                b, free = filled(l, "NROW2")
                                V.tensor_copy(rs2[:], b[:]).then_inc(free, 1)
                        else:
                            k = pos - 8
                            a, free = done(l, M0, q, pos)
                            V.tensor_tensor(T[2], a[:], rs2[:], ALU.mult).then_inc(free, 1)
                            V.drain()
                            V.tensor_tensor(xT[:, k, :], xT[:, k, :], T[2], ALU.add)
                            if final:
                                V.drain().then_inc(x_upd, 1)
                                norm_tile(l * 16 + (16 + k), k, nw[:, bass.ds(l * KT + (KT + k), 1)])

                mlp_quarter(0, first=True)
                with dve.Fori(1, QUARTERS - 1) as q:
                    mlp_quarter(q)
                mlp_quarter(QUARTERS - 1, final=True)
            for e in range(2 * TT):
                t, half = e // 2, e % 2
                dve.wait_ge(bank_full, DEPTH * N_FILLS + XF + e + 1)
                V.tensor_copy(x_tok[:, t, half * 512:(half + 1) * 512], bank[e % 4][:]).then_inc(bank_free[e % 4], 1)
                V.drain().then_inc(out_copied, 1)


def constants():
    c = np.zeros((P, N_CONST), np.float32)
    p = np.arange(P)
    c[p, CC["ident"] + p] = 1.0
    c[:, CC["ones"]] = 1.0
    c[:, CC["blk"]:CC["blk"] + 2] = p[:, None] // SWA_DIM == np.arange(2)[None, :]
    c[:, CC["sign"]] = np.where(p % SWA_DIM < ROPE_HALF, -1.0, 1.0)
    half = ROPE_HALF
    c[:, CC["scan"]:CC["scan"] + SEQ] = np.arange(SEQ) % GLA_CHUNK != 0
    key = np.arange(2 * P)[None, :]
    c[:, CC["swam"]:CC["swam"] + 2 * P] = np.where((key > p[:, None]) & (key <= p[:, None] + P), 0.0, -3.0e38)
    freq = np.float32(500000.0) ** (-np.arange(0, 2 * half, 2, dtype=np.float32) / np.float32(2 * half))
    c[:, CC["invf"]] = np.where(p % SWA_DIM < 2 * half, freq[p % half], 0.0)
    g = (p[None, :] >= p[:, None]) & (p[None, :] // GLA_CHUNK == p[:, None] // GLA_CHUNK)
    return c, g.astype(np.int32)


def kernel(**inputs):
    import concourse.bacc as _bacc
    from concourse.bass_utils import run_bass_kernel_spmd as _run

    a = {k: np.asarray(v) for k, v in inputs.items()}

    def cols(w):
        return w.reshape(DEPTH, -1, P).transpose(0, 2, 1)

    sinks = a["sinks"].reshape(DEPTH, SWA_KV, 2, 2).transpose(0, 1, 3, 2).reshape(DEPTH, 1, SWA_HEADS)
    params = np.concatenate([
        cols(a["conv_w"].reshape(DEPTH, -1)), cols(a["conv_b"]),
        cols(a["gla_ba"]), cols(a["gla_onorm_w"]), cols(np.tile(a["q_norm_w"], (1, 2))),
        cols(np.tile(a["k_norm_w"], (1, 2))), np.broadcast_to(sinks, (DEPTH, P, SWA_HEADS))], axis=2)
    norms = np.concatenate([a["norm1_w"], a["norm2_w"]]).reshape(2 * DEPTH * KT, P).T
    consts, gmask = constants()
    feed = dict(x=a["x"], positions=a["positions"][0], params=params, w_in=a["w_in"], gla_wa2=a["gla_wa2"],
                w_branch=a["w_branch"], w_o=a["w_o"], w_up=a["w_up"], w_down=a["w_down"],
                norms=norms, consts=consts, gmask=gmask)
    nc = _bacc.Bacc("TRN2", target_bir_lowering=False, num_devices=1)
    arrays, args = {}, []
    for name, value in feed.items():
        value = np.ascontiguousarray(value)
        arrays[f"in_{name}_dram"] = value
        args.append(nc.dram_tensor(f"in_{name}_dram", value.shape, mybir.dt.from_np(value.dtype), kind="ExternalInput").ap())
    args.append(nc.dram_tensor("out_0_dram", (1, SEQ, D_MODEL), mybir.dt.float32, kind="ExternalOutput").ap())
    hybrid_trunk(nc, *args)
    r = _run(nc, [arrays], core_ids=[0])
    return r.results[0]["out_0_dram"]
```

```python
import concourse.bass as bass
from concourse import mybir
from contextlib import ExitStack
import numpy as np

D_MODEL, SEQ, DEPTH = 1024, 512, 2
P = 128
KT = D_MODEL // P
TT = SEQ // P
CONV_DIM, GLA_HEADS, GLA_DK, GLA_DV, GLA_RANK, GLA_CHUNK = 512, 4, 64, 128, 16, 64
SWA_HEADS, SWA_KV, SWA_DIM = 8, 2, 64
N_BRANCH, BRANCH_W, D_FF = 3, 512, 4096
BK = BRANCH_W // P
CHUNKS = SEQ // GLA_CHUNK
EPS = 1e-6
SIZES = dict(cx=CONV_DIM, cb=CONV_DIM, cc=CONV_DIM, gq=256, gk=256, gv=512, gr=512, ga=GLA_RANK,
             sq=512, sk=128, sv=128, gates=N_BRANCH * D_MODEL)
COL = {}
for _name, _n in SIZES.items():
    COL[_name] = sum(SIZES[x] for x in list(SIZES)[:len(COL)])

SLAB_COLS = 256
UNIT_NAMES = (["ga", "void"] + [f"gq{i}" for i in range(2)] + [f"gk{i}" for i in range(2)]
              + [f"sq{i}" for i in range(4)] + ["sk0", "sv0"] + [f"gv{i}" for i in range(4)]
              + [f"cx{i}" for i in range(4)] + [f"cc{i}" for i in range(4)]
              + [f"cb{i}" for i in range(4)] + [f"gr{i}" for i in range(4)])
UNIT = {n: i for i, n in enumerate(UNIT_NAMES)}
PROJ_UNITS = len(UNIT_NAMES)
GATE_IT, MLP_IT = 16, 16
G0 = PROJ_UNITS
O0 = G0 + N_BRANCH * GATE_IT
M0 = O0 + KT
QUARTERS = 4
UNITS = M0 + QUARTERS * MLP_IT
SLABS = PROJ_UNITS // 2 + N_BRANCH * 6 + 4 + QUARTERS * 8
HALF_SLABS = SLABS // 2
SPLIT = 4
AHEAD = 3
GATE_SLAB = [0, 0, 1, 1, 2, 2, 2, 2, 3, 3, 4, 4, 5, 5, 5, 5]

SEQUENCE = """ga NSUM gq0 NROW gq1 ZA gk0 ZB gk1 sq0 sq1 X0 X1 sq2 sq3 KT0 KT1 ATT0 sk0 ATT1 sv0 QSUM gv0 QW
VS0 QN4 gv1 VT0 QN0 gv2 VT1 QN1 KV0 gv3 VT2 SC0 QN2 cx0 VT3 GO0 SM0 SC1 cx1 ATT2 GO1 PT0 SM1 SC2
KV1 QN3 cx2 ATT3 GO2 PV0 PT1 SM2 SC3 cx3 GO3 PV1 PT2 SM3 cc0 OSUM PV2 PT3 SC4 cc1 SM4 SC5 ON0
cc2 PV3 PT4 SM5 SC6 ON1 cc3 PV4 PT5 SM6 SC7 ON2 cb0 PV5 PT6 SM7 ON3 cb1 PV6 PT7 cb2 PV7 cb3 gr0
gr1 gr2 gr3""".split()


def step_of(word):
    return word.rstrip("0123456789"), int("0" + word[len(word.rstrip("0123456789")):])


SPLIT_AT, SPLIT_WITHIN = {}, {}
_previous = 0
for _n, _word in enumerate(SEQUENCE):
    if _word in UNIT:
        _early = any(w.startswith("SC") for w in SEQUENCE[_previous + 1:_n])
        if _word in ("gr1", "gr2", "gr3"):
            SPLIT_WITHIN[_previous] = UNIT[_word]
        else:
            SPLIT_AT[_previous + 1 if _early else _n] = UNIT[_word]
        _previous = _n

FILLS = []
for _word in SEQUENCE:
    _kind, _i = step_of(_word)
    if _word in UNIT:
        continue
    if _kind in ("KV", "SC", "ZA"):
        FILLS += [f"{_word}a", f"{_word}b"]
    elif _kind == "PT":
        FILLS += [f"{_word}cur"] if _i % TT == 0 else [f"{_word}prev", f"{_word}cur"]
    elif _kind not in ("X", "ZB", "SM", "QW"):
        FILLS.append(_word)
FILLS += ["NSUM2", "NROW2"]
FILL = {n: i for i, n in enumerate(FILLS)}
N_FILLS = len(FILLS)
XF = KT


def bank_fills(b, before=N_FILLS):
    return sum(1 for i in range(before) if i % 4 == b)


PC = dict(cw=0, cb=12, ba=16, on=18, qn=19, kn=20, sink=21)
N_PARAMS = 29
CC = dict(ident=0, invf=128, ones=129, blk=130, sign=132, scan=133, swam=645)
N_CONST = 901
HEADS_Q = SWA_HEADS + SWA_KV

QN_ORDER = [4, 0, 1, 2, 3]

ROPE_HALF = SWA_DIM // 4 // 2
ROPE_SWAP = [(i + ROPE_HALF) % (2 * ROPE_HALF) if i < 2 * ROPE_HALF else i for i in range(32)]

TWO_PI = 6.283185307179586
PI_1, PI_2 = 6.28125, 0.001934051513671875
PI_3 = TWO_PI - PI_1 - PI_2
ROUND = 1.5 * 2.0 ** 23


def hybrid_trunk(nc, x, positions, params, w_in, gla_wa2, w_branch, w_o, w_up, w_down, norms, consts, gmask, out):
    f32, f32r, i32 = mybir.dt.float32, mybir.dt.float32r, mybir.dt.int32
    ALU, ACT, AX = mybir.AluOpType, mybir.ActivationFunctionType, mybir.AxisListType
    ctx = ExitStack()
    with ctx:
        TILE = 2048
        BASE = -(-nc.sbuf_base // 64) * 64

        def at(name, tile, shape, dt=f32, extra=0):
            return nc.alloc_sbuf_tensor_at(name, [P] + shape, dt, offset=BASE + tile * TILE + extra)

        xT = at("xT", 0, [KT, SEQ])
        uh = at("uh", 8, [KT, SEQ], f32r)
        ul = at("ul", 16, [KT, SEQ], f32r)
        raw = [at(f"raw{i}", 24 + 4 * i, [KT, SLAB_COLS]) for i in range(2)]
        raw4 = [at(f"raw_branch{i}", 24 + 4 * i, [BK, 2 * SLAB_COLS]) for i in range(2)]
        raw_ga = at("raw_ga", 24, [KT, GLA_RANK])
        wh = [at(f"wh{i}", 32 + 2 * i, [KT, P], f32r) for i in range(SPLIT)]
        wl = [at(f"wl{i}", 40 + 2 * i, [KT, P], f32r) for i in range(SPLIT)]
        yh = at("yh", 48, [12, SEQ], f32r)
        yl = at("yl", 60, [12, SEQ], f32r)
        S = at("gla_states", 48, [2, CHUNKS, P])
        vT = at("gla_v_tokens", 60, [GLA_HEADS, TT, P])
        gq = at("gla_q", 52, [2, SEQ])
        gk = at("gla_k", 54, [2, SEQ])
        kin = at("gla_k_in", 56, [2, SEQ])
        gb = at("gla_b", 58, [2, SEQ])
        eb = at("gla_exp_b", 64, [2, SEQ])
        vtmp = at("v_features", 66, [2, SEQ])
        kendT = at("gla_k_end_tokens", 68, [2, TT, P])
        attm = at("gla_att", 70, [2, TT, P])
        mixed = at("mixed", 72, [KT, SEQ])
        x_tok = at("x_tokens", 72, [TT, D_MODEL])
        cu = at("conv_u", 72, [4, SEQ])
        sm = [at(f"probs{i}", (94, 76)[i], [4, 2 * P]) for i in range(2)]
        pT = at("probs_keys", 78, [2, 4, P])
        yo = at("gla_o", 80, [4, SEQ])
        gt = at("gate_tanh", 80, [4, SEQ])
        sq = at("swa_q", 84, [4, SEQ])
        pos_i = at("positions_i", 84, [SEQ], i32)
        kd = at("swa_k_twice", 88, [2, SEQ])
        vd = at("swa_v_twice", 90, [2, TT, 2, SWA_DIM])
        cosT = at("rope_cos", 92, [SEQ])
        sinT = at("rope_sin", 93, [SEQ])
        ct = at("conv_y", 94, [SEQ])
        T3 = at("temps", 95, [3, SEQ])
        T = [T3[:, i, :] for i in range(3)]
        rs_sq = T[2]
        nacc = at("norm_sum", 98, [SEQ])
        rs = at("rsqrt_rows", 99, [SEQ])
        gaT = at("gla_a", 64, [SEQ])
        rs2 = at("rsqrt_rows_mlp", 94, [SEQ])
        sqr = at("squares", 76, [4, SEQ])
        sqk = at("squares_k", 98, [SEQ])
        sqo = [at(f"squares_o{i}", (54, 55, 58, 59)[i], [SEQ]) for i in range(GLA_HEADS)]
        conv = [at(f"conv_taps{i}", (98, 96)[i], [SEQ]) for i in range(2)]
        wide = [at(f"norm_columns{i}", (72, 73, 74, 83, 75)[i], [TT, 2, SWA_DIM]) for i in range(5)]
        cst = at("consts", 100, [N_CONST])
        o = 100 * TILE + 4 * N_CONST
        gm = nc.alloc_sbuf_tensor_at("gla_mask", [P, P], i32, offset=BASE + o + (-o) % 64)
        o = o + (-o) % 64 + 512
        par = nc.alloc_sbuf_tensor_at("params", [P, N_PARAMS], f32, offset=BASE + o)
        o += 192
        wa2 = nc.alloc_sbuf_tensor_at("wa2", [GLA_RANK, 256], f32, offset=BASE + o)
        o += 1024
        small = nc.alloc_sbuf_tensor_at("small", [P, 64], f32, offset=BASE + o)
        o += 256
        nw = nc.alloc_sbuf_tensor_at("norm_weights", [P, 2 * DEPTH * KT], f32, offset=BASE + o)
        o += 128
        stat = nc.alloc_sbuf_tensor_at("stat", [P, 4, TT * HEADS_Q], f32, offset=BASE + o)
        o += 16 * TT * HEADS_Q
        stat_i = nc.alloc_sbuf_tensor_at("stat_bits", [P, TT * HEADS_Q], i32, offset=BASE + o)
        ident, ones, blk = cst[:, 0:P], cst[:, CC["ones"]:CC["ones"] + 1], cst[:, CC["blk"]:CC["blk"] + 2]
        scanm = cst[:, CC["scan"]:CC["scan"] + SEQ]
        swam = cst[:, CC["swam"]:CC["swam"] + 2 * P]
        invf, sign = cst[:, CC["invf"]:CC["invf"] + 1], cst[:, CC["sign"]:CC["sign"] + 1]
        neg4, d4, sum4, es4, den4 = ([small[:, 8 * i + 4 * j:8 * i + 4 * j + 4] for j in range(2)] for i in range(5))
        m4, qn8, one_col, zero_col = small[:, 40:44], small[:, 44:45], small[:, 45:46], small[:, 46:47]

        acc = [ctx.enter_context(nc.psum_tensor(f"acc{i}", [P, SEQ], f32)) for i in range(4)]
        bank = [ctx.enter_context(nc.psum_tensor(f"bank{i}", [P, SEQ], f32)) for i in range(4)]

        def sem(name):
            return ctx.enter_context(nc.semaphore(name))

        in_full, masks_full, pos_full, gm_full, nw_full, par_full, out_full = map(
            sem, "in_full masks_full pos_full gm_full nw_full par_full out_full".split())
        x_full = [sem(f"x_full{i}") for i in range(TT)]
        raw_full = [sem(f"raw_full{i}") for i in range(2)]
        raw_free = [sem(f"raw_free{i}") for i in range(2)]
        acc_free = [sem(f"acc_free{i}") for i in range(4)]
        bank_free = [sem(f"bank_free{i}") for i in range(4)]
        (par_free, hi_done, lo_done, unit_done, bank_full, ready0, ga_ready, z_biased, softplus_ready,
         b_ready, gla_exps, gla_qk, gv_ready, sv_ready, vT_ready, kendT_ready, att_ready,
         states_ready, yo_ready, yo_sq, swa_raw, swa_sq, stat_ready, wide_ready, swa_roped, vs_ready, y_val,
         y_hi, yconv_ready, ygla_ready, gr_scaled, gr_tanh, pv_hi, yswa_ready, scores_ready, exps_ready, den_ready,
         probs_ready, pprev_ready, pcur_ready, gate_scaled, gate_ready, mixed_done, mx_hi, mx_ready, x_odd, x_upd,
         x_sq, x_acc, u_hi, u_ready, relu_ready, hid_val, hid_hi, hid_ready, angle_ready, sines_ready,
         out_copied) = map(sem, """
         par_free hi_done lo_done unit_done bank_full ready0 ga_ready z_biased softplus_ready b_ready
         gla_exps gla_qk gv_ready sv_ready vT_ready kendT_ready att_ready states_ready yo_ready
         yo_sq swa_raw swa_sq stat_ready wide_ready swa_roped vs_ready y_val y_hi yconv_ready ygla_ready
         gr_scaled gr_tanh pv_hi yswa_ready scores_ready exps_ready den_ready probs_ready pprev_ready pcur_ready
         gate_scaled gate_ready mixed_done mx_hi mx_ready x_odd x_upd x_sq x_acc u_hi u_ready relu_ready hid_val
         hid_hi hid_ready angle_ready sines_ready out_copied""".split())
        UNIT_CREDIT, HID_CREDIT = SPLIT, 2

        def unit_index(base, it, pos):
            return it * 16 + (base + pos)

        def slab_half(base, it, pos):
            if base == G0:
                return it * 3 + (G0 // 4 + GATE_SLAB[pos] // 2)
            if base == M0:
                return it * 4 + (19 + pos // 4)
            return (pos // 4) + (17 if base == O0 else 0)

        def slab_slot(base, pos):
            return GATE_SLAB[pos] % 2 if base == G0 else pos // 2 % 2

        def slab_ends(base, pos):
            if base == G0:
                return pos % 16 in (1, 3, 7, 9, 11, 15)
            return pos % 2 == 1

        def k_tiles(base, pos):
            return BK if base == G0 and pos % 8 >= 4 else KT

        def raw_view(base, pos):
            slot = slab_slot(base, pos)
            if base == 0 and pos == 0:
                return raw_ga[:]
            if k_tiles(base, pos) == BK:
                return raw4[slot][:, :, pos % 4 * P:pos % 4 * P + P]
            return raw[slot][:, :, pos % 2 * P:pos % 2 * P + P]

        def split_view(w, base, pos):
            if base == 0 and pos == 0:
                return w[0][:, :, 0:GLA_RANK]
            return w[pos % SPLIT][:, 0:k_tiles(base, pos), :]

        def ahead(base, it, pos):
            pos += AHEAD
            if base == 0 and pos >= PROJ_UNITS:
                return G0, 0, pos - PROJ_UNITS
            if base == G0 and pos >= GATE_IT:
                return G0, it + 1, pos - GATE_IT
            if base == O0 and pos >= KT:
                return M0, 0, pos - KT
            if base == M0 and pos >= MLP_IT:
                return M0, it + 1, pos - MLP_IT
            return base, it, pos

        def splits_in_last_quarter(l, pos):
            if pos + AHEAD < MLP_IT:
                return [(l, *ahead(M0, QUARTERS - 1, pos))]
            return [(l + 1, 0, 0, pos + AHEAD - MLP_IT)] if pos + AHEAD - MLP_IT != 1 else []

        block = ctx.enter_context(nc.Block())

        @block.sync
        def _(sp):
            sp.dma_start(cst[:, 0:CC["scan"]], consts[:, 0:CC["scan"]]).then_inc(in_full, 16)
            for t in range(TT):
                sp.dma_start(x_tok[:, t, :], x[0, t * P:(t + 1) * P, :]).then_inc(x_full[t], 16)

            sp.dma_start(cst[:, CC["scan"]:], consts[:, CC["scan"]:]).then_inc(masks_full, 16)

            def load(l, base, it, pos, source, into=None):
                slot = slab_slot(base, pos)
                uses = sp.to_reg(l * HALF_SLABS + slab_half(base, it, pos) + 1)
                sp.wait_ge(in_full, 16)
                sp.wait_ge(raw_free[slot], uses)
                sp.dma_start(raw[slot][:] if into is None else into, source).then_inc(raw_full[slot], 16)

            def rows(w, l, first, k, col, n):
                return w[bass.ds(l, 1), first:first + k * P, col:col + n].rearrange(
                    "o (k p) n -> p (o k) n", p=P)

            def layer_first(l):
                sp.wait_ge(in_full, 16)
                sp.wait_ge(par_free, l + 1)
                sp.dma_start(par[:], params[bass.ds(l, 1)].rearrange("o p n -> p (o n)")).then_inc(par_full, 16)
                sp.dma_start(wa2[:], gla_wa2[bass.ds(l, 1)].rearrange("o p n -> p (o n)")).then_inc(par_full, 16)
                load(l, 0, 0, 0, rows(w_in, l, 0, KT, COL["ga"], GLA_RANK), raw_ga[:])
                project(l, 2)

            def project(l, pos):
                kind, i = step_of(UNIT_NAMES[pos])
                load(l, 0, 0, pos, rows(w_in, l, 0, KT, COL[kind] + i * P, SLAB_COLS))

            def layer_rest(l):
                for pos in range(4, PROJ_UNITS, 2):
                    project(l, pos)
                with sp.Fori(0, N_BRANCH) as g:
                    wg = w_in[bass.ds(l, 1), :, COL["gates"]:].rearrange(
                        "o (k p) (g n) -> p (o k) g n", p=P, g=N_BRANCH)
                    wb = w_branch[bass.ds(l, 1)].rearrange("o g (k p) n -> p (o g) k n", p=P)
                    for half in range(2):
                        for s in range(2):
                            col = 512 * half + SLAB_COLS * s
                            load(l, G0, g, 8 * half + 2 * s, wg[:, :, bass.ds(g, 1), col:col + SLAB_COLS]
                                 .rearrange("p k g n -> p k (g n)"))
                        load(l, G0, g, 8 * half + 4, wb[:, bass.ds(g, 1), :, 512 * half:512 * half + 512]
                             .rearrange("p g k n -> p (g k) n"), raw4[slab_slot(G0, 8 * half + 4)][:])
                for s in range(4):
                    load(l, O0, 0, 2 * s, rows(w_o, l, 0, KT, SLAB_COLS * s, SLAB_COLS))
                with sp.Fori(0, QUARTERS) as q:
                    up = w_up[bass.ds(l, 1)].rearrange("o (k p) (q n) -> p (o k) q n", p=P, q=QUARTERS)
                    down = w_down[bass.ds(l, 1)].rearrange("o (q k p) n -> p (o q) k n", p=P, q=QUARTERS)
                    for s in range(4):
                        load(l, M0, q, 2 * s, up[:, :, bass.ds(q, 1), SLAB_COLS * s:SLAB_COLS * (s + 1)]
                             .rearrange("p k q n -> p k (q n)"))
                    for s in range(4):
                        load(l, M0, q, 8 + 2 * s, down[:, bass.ds(q, 1), :, SLAB_COLS * s:SLAB_COLS * (s + 1)]
                             .rearrange("p q k n -> p (q k) n"))

            layer_first(0)
            with sp.Fori(0, DEPTH - 1) as l:
                layer_rest(l)
                layer_first(l + 1)
            layer_rest(DEPTH - 1)
            load(DEPTH, 0, 0, 0, rows(w_in, DEPTH - 1, 0, KT, COL["ga"], GLA_RANK), raw_ga[:])
            sp.wait_ge(raw_free[1], DEPTH * HALF_SLABS + 1)
            sp.sem_inc(raw_full[1], 16)
            for t in range(TT):
                sp.wait_ge(out_copied, 2 * t + 2)
                sp.dma_start(out[0, t * P:(t + 1) * P, :], x_tok[:, t, :]).then_inc(out_full, 16)
            sp.wait_ge(out_full, 16 * TT)

        @block.tensor
        def _(pe):
            pe.sem_inc(unit_done, UNIT_CREDIT)
            pe.wait_ge(ready0, 1)

            def open_bank(l, name, plain=False, waits=()):
                f = FILL[name]
                uses = pe.to_reg(l * bank_fills(f % 4) + (bank_fills(f % 4, f) + XF // 4 + 1))
                waits = [(semaphore, pe.to_reg(count)) for semaphore, count in waits]
                if plain:
                    pe.wait_ge(in_full, 16)
                pe.wait_ge(bank_free[f % 4], uses)
                for semaphore, count in waits:
                    pe.wait_ge(semaphore, count)
                return bank[f % 4]

            def open_unit(l, base, it, pos):
                u, b = unit_index(base, it, pos), (base + pos) % 4
                pe.wait_ge(lo_done, l * UNITS + u + 1)
                pe.wait_ge(acc_free[b], l * (UNITS // 4) + it * 4 + (base + pos) // 4 + 1)

            def products(base, pos, k, right_h, right_l):
                b, n = (base + pos) % 4, k_tiles(base, pos)
                h, lo = split_view(wh, base, pos), split_view(wl, base, pos)
                m = GLA_RANK if base == 0 and pos == 0 else P
                nc.tensor.matmul(acc[b][0:m, :], h[:, k, :], right_h(k), start=k == 0, stop=False)
                nc.tensor.matmul(acc[b][0:m, :], h[:, k, :], right_l(k), start=False, stop=False)
                return nc.tensor.matmul(acc[b][0:m, :], lo[:, k, :], right_h(k), start=False, stop=k == n - 1)

            def unit(l, base, it, pos, right_h, right_l, ready=None, ready_at=None, gate=None):
                open_unit(l, base, it, pos)
                if gate is not None:
                    gate()
                for k in range(k_tiles(base, pos)):
                    if ready is not None:
                        pe.wait_ge(ready, ready_at(k))
                    last = products(base, pos, k, right_h, right_l)
                last.then_inc(unit_done, 2 if base == 0 and pos == 0 else 1)

            def two_units(l, base, it, pos, right_h, right_l, ready, ready_at):
                for p in (pos, pos + 1):
                    open_unit(l, base, it, p)
                    for k in range(KT - 1):
                        if p == pos:
                            pe.wait_ge(ready, ready_at(k))
                        products(base, p, k, right_h, right_l)
                pe.wait_ge(ready, ready_at(KT - 1))
                for p in (pos, pos + 1):
                    products(base, p, KT - 1, right_h, right_l).then_inc(unit_done, 1)

            def u_tile(t):
                return lambda k: t[:, k, :]

            pe.wait_ge(in_full, 16)
            for t in range(TT):
                pe.wait_ge(x_full[t], 16)
            for k in range(KT):
                pe.wait_ge(bank_free[k % 4], k // 4 + 1)
                for t in range(TT):
                    last = nc.tensor.transpose(bank[k % 4][:, t * P:(t + 1) * P], x_tok[:, t, k * P:(k + 1) * P], ident)
                last.then_inc(bank_full, 1)

            def sum_squares(l, name, first):
                b = open_bank(l, name)
                pe.wait_ge(x_acc, l * 16 + first + 8)
                for t in range(TT):
                    last = nc.tensor.matmul(b[:, t:t + 1], nacc[:, t * P:(t + 1) * P], ones, start=True, stop=True)
                last.then_inc(bank_full, 1)

            def rows(l, name, ready_at, result, column):
                b = open_bank(l, name)
                pe.wait_ge(stat_ready, l * 4 + ready_at)
                for t in range(TT):
                    last = nc.tensor.transpose(b[:, t * P:(t + 1) * P],
                                               stat[:, result, column(t):column(t) + 1].broadcast_to([P, P]), ident)
                last.then_inc(bank_full, 1)

            with pe.Fori(0, DEPTH) as l:
                for word in SEQUENCE:
                    kind, i = step_of(word)
                    if word in UNIT or word == "ga":
                        pos = UNIT[word]
                        if word == "ga":
                            unit(l, 0, 0, pos, u_tile(uh), u_tile(ul), u_ready, lambda k: l * 16 + k + 1)
                        else:
                            unit(l, 0, 0, pos, u_tile(uh), u_tile(ul))
                    elif kind == "NSUM":
                        sum_squares(l, word, 0)
                    elif kind == "NROW":
                        rows(l, word, 1, 1, lambda t: t)
                    elif kind == "ZA":
                        for pair in range(2):
                            b = open_bank(l, word + "ab"[pair])
                            pe.wait_ge(ga_ready, l + 1)
                            nc.tensor.matmul(b[:], wa2[:, pair * P:(pair + 1) * P], gaT[0:GLA_RANK, :],
                                             start=True, stop=True).then_inc(bank_full, 1)
                    elif kind == "VT":
                        b = open_bank(l, word)
                        pe.wait_ge(gv_ready, l * 4 + i + 1)
                        for t in range(TT):
                            last = nc.tensor.transpose(b[:, t * P:(t + 1) * P], vtmp[:, (i + 1) % 2, t * P:(t + 1) * P], ident)
                        last.then_inc(bank_full, 1)
                    elif kind == "KT":
                        b = open_bank(l, word)
                        pe.wait_ge(gla_qk, l * 2 + i + 1)
                        for t in range(TT):
                            last = nc.tensor.transpose(b[:, t * P:(t + 1) * P], gk[:, i, t * P:(t + 1) * P], ident)
                        last.then_inc(bank_full, 1)
                    elif kind == "ATT":
                        b = open_bank(l, word)
                        pe.wait_ge(gla_qk, l * 2 + i // 2 + 1)
                        r = GLA_DK * (i % 2)
                        for t in range(TT):
                            s = slice(t * P, (t + 1) * P)
                            last = nc.tensor.matmul(b[:, s], kin[r:r + GLA_DK, i // 2, s], gq[r:r + GLA_DK, i // 2, s],
                                                    start=True, stop=True)
                        last.then_inc(bank_full, 1)
                    elif kind == "KV":
                        for odd in range(2):
                            b = open_bank(l, word + "ab"[odd], True, waits=[] if odd else
                                          [(kendT_ready, l * 2 + i + 1), (vT_ready, l * 4 + 2 * i + 2)])
                            r = GLA_CHUNK * odd
                            for h in range(2):
                                for t in range(TT):
                                    last = nc.tensor.matmul(
                                        b[GLA_DK * h:GLA_DK * (h + 1), t * P:(t + 1) * P],
                                        kendT[r:r + GLA_CHUNK, i, t, GLA_DK * h:GLA_DK * (h + 1)],
                                        vT[r:r + GLA_CHUNK, 2 * i + h, t, :], start=True, stop=True)
                            last.then_inc(bank_full, 1)
                    elif kind == "GO":
                        b = open_bank(l, word)
                        pe.wait_ge(att_ready, l * 4 + i + 1)
                        pe.wait_ge(vT_ready, l * 4 + i + 1)
                        pe.wait_ge(states_ready, l * 2 + i // 2 + 1)
                        r = GLA_DK * (i % 2)
                        for t in range(TT):
                            nc.tensor.matmul(b[:, t * P:(t + 1) * P], vT[:, i, t, :], attm[:, i % 2, t, :],
                                             start=True, stop=False)
                            for c in (2 * t, 2 * t + 1):
                                if c:
                                    s = slice(c * GLA_CHUNK, (c + 1) * GLA_CHUNK)
                                    last = nc.tensor.matmul(b[:, s], S[r:r + GLA_DK, i // 2, c - 1, :],
                                                            gq[r:r + GLA_DK, i // 2, s], start=False,
                                                            stop=c == 2 * t + 1)
                        last.then_inc(bank_full, 1)
                    elif kind == "QSUM":
                        b = open_bank(l, word)
                        pe.wait_ge(swa_sq, l * 5 + 5)
                        for i in range(5):
                            source = sqk[:] if i == 4 else sqr[:, i, :]
                            for t in range(TT):
                                last = nc.tensor.matmul(b[:, HEADS_Q * t + 2 * i:HEADS_Q * t + 2 * i + 2],
                                                        source[:, t * P:(t + 1) * P], blk, start=True, stop=True)
                        last.then_inc(bank_full, 1)
                    elif kind == "OSUM":
                        b = open_bank(l, word)
                        pe.wait_ge(yo_sq, l * 4 + 4)
                        for h in range(GLA_HEADS):
                            for t in range(TT):
                                last = nc.tensor.matmul(b[:, GLA_HEADS * t + h:GLA_HEADS * t + h + 1],
                                                        sqo[h][:, t * P:(t + 1) * P], ones, start=True, stop=True)
                        last.then_inc(bank_full, 1)
                    elif kind == "QN":
                        b = open_bank(l, word)
                        pe.wait_ge(wide_ready, l * 5 + QN_ORDER.index(i) + 1)
                        for t in range(TT):
                            last = nc.tensor.transpose(b[:, t * P:(t + 1) * P],
                                                       wide[i][:, t].rearrange("p h d -> p (h d)"), ident)
                        last.then_inc(bank_full, 1)
                    elif kind == "ON":
                        rows(l, word, 3, 3, lambda t: GLA_HEADS * t + i)
                    elif kind == "VS":
                        b = open_bank(l, word)
                        pe.wait_ge(sv_ready, l + 1)
                        for t in range(TT):
                            last = nc.tensor.transpose(b[:, t * P:(t + 1) * P], vtmp[:, 0, t * P:(t + 1) * P], ident)
                        last.then_inc(bank_full, 1)
                    elif kind == "SC":
                        kv, n = i // TT, i % TT
                        pe.wait_ge(swa_roped, l * 5 + 3 + 2 * kv)
                        for odd in range(2):
                            b = open_bank(l, word + "ab"[odd])
                            r = SWA_DIM * odd
                            first = 0 if n else P
                            for j in range(2):
                                last = nc.tensor.matmul(
                                    b[:, j * 2 * P + first:(j + 1) * 2 * P],
                                    sq[r:r + SWA_DIM, 2 * kv + j, n * P:(n + 1) * P],
                                    kd[r:r + SWA_DIM, kv, (n - 1) * P + first:(n + 1) * P], start=True, stop=True)
                            last.then_inc(bank_full, 1)
                    elif kind == "PT":
                        pe.wait_ge(probs_ready, l * 8 + i + 1)
                        for cur in ((0, 1) if i % TT else (1,)):
                            b = open_bank(l, word + ("cur" if cur else "prev"))
                            for h in range(4):
                                last = nc.tensor.transpose(b[:, h * P:(h + 1) * P], sm[i % 2][:, h, cur * P:(cur + 1) * P], ident)
                            last.then_inc(bank_full, 1)
                    elif kind == "PV":
                        kv, n = i // TT, i % TT
                        b = open_bank(l, word)
                        pe.wait_ge(vs_ready, l + 1)
                        if n:
                            pe.wait_ge(pprev_ready, l * 6 + kv * 3 + n)
                            nc.tensor.matmul(b[:], vd[:, kv, n - 1].rearrange("p a d -> p (a d)"),
                                             pT[:, 0].rearrange("p h c -> p (h c)"), start=True, stop=False)
                        pe.wait_ge(pcur_ready, l * 8 + i + 1)
                        nc.tensor.matmul(b[:], vd[:, kv, n].rearrange("p a d -> p (a d)"),
                                         pT[:, 1].rearrange("p h c -> p (h c)"), start=n == 0,
                                         stop=True).then_inc(bank_full, 1)
                with pe.Fori(0, N_BRANCH) as g:
                    for pos in range(GATE_IT):
                        if pos % 8 < 4:
                            unit(l, G0, g, pos, u_tile(uh), u_tile(ul))
                        else:
                            def branches_ready():
                                pe.wait_ge(yconv_ready, l * 4 + 4)
                                pe.wait_ge(ygla_ready, l * 4 + 4)
                                pe.wait_ge(yswa_ready, l * 8 + 8)

                            def y_tile(t):
                                return lambda k: t[:, bass.ds(g * BK + k, 1), :].rearrange("p a n -> p (a n)")
                            unit(l, G0, g, pos, y_tile(yh), y_tile(yl), gate=branches_ready if pos == 4 else None)
                for pos in range(KT):
                    if pos == 0:
                        two_units(l, O0, 0, pos, u_tile(yh), u_tile(yl), mx_ready, lambda k: l * 8 + k + 1)
                    elif pos > 1:
                        unit(l, O0, 0, pos, u_tile(yh), u_tile(yl))

                def mlp_quarter(q, first):
                    for pos in range(MLP_IT):
                        if pos == 0 and first:
                            unit(l, M0, q, pos, u_tile(uh), u_tile(ul), u_ready, lambda k: l * 16 + 8 + k + 1)
                        elif pos < 8:
                            unit(l, M0, q, pos, u_tile(uh), u_tile(ul))
                            if pos == 1 and first:
                                sum_squares(l, "NSUM2", 8)
                            if pos == 3 and first:
                                rows(l, "NROW2", 4, 1, lambda t: t)
                        elif pos == 8:
                            unit(l, M0, q, pos, u_tile(yh), u_tile(yl), hid_ready,
                                 lambda k: l * 32 + q * 8 + (k + 1 + HID_CREDIT))
                        else:
                            unit(l, M0, q, pos, u_tile(yh), u_tile(yl))

                mlp_quarter(0, True)
                with pe.Fori(1, QUARTERS) as q:
                    mlp_quarter(q, False)
            pe.wait_ge(x_upd, 8 + 16 * DEPTH)
            for e in range(2 * TT):
                t, half = e // 2, e % 2
                pe.wait_ge(bank_free[e % 4], DEPTH * bank_fills(e % 4) + XF // 4 + e // 4 + 1)
                for j in range(4):
                    last = nc.tensor.transpose(bank[e % 4][:, j * P:(j + 1) * P], xT[:, 4 * half + j, t * P:(t + 1) * P], ident)
                last.then_inc(bank_full, 1)

        @block.scalar
        def _(act):
            act.dma_start(pos_i[:], positions.partition_broadcast(P)).then_inc(pos_full, 16)
            act.dma_start(nw[:], norms).then_inc(nw_full, 16)
            act.dma_start(gm[:], gmask).then_inc(gm_full, 16)

            def filled(l, name):
                f = FILL[name]
                act.wait_ge(bank_full, l * N_FILLS + XF + f + 1)
                return bank[f % 4], bank_free[f % 4]

            def split_high(l, base, it, pos):
                act.wait_ge(raw_full[slab_slot(base, pos)], (l * HALF_SLABS + slab_half(base, it, pos)) * 16 + 16)
                act.wait_ge(unit_done, l * UNITS + unit_index(base, it, pos) + 1)
                nc.scalar.activation(split_view(wh, base, pos), raw_view(base, pos), ACT.Copy).then_inc(
                    hi_done, 2 if base == 0 and pos == 0 else 1)

            def done(l, base, it, pos):
                act.wait_ge(unit_done, l * UNITS + unit_index(base, it, pos) + 1 + UNIT_CREDIT)
                return acc[(base + pos) % 4], acc_free[(base + pos) % 4]

            def norm_high(k, weight):
                nc.scalar.activation(uh[:, k, :], xT[:, k, :], ACT.Copy, scale=weight).then_inc(u_hi, 1)

            def norm_square(e, k, temp_free=False):
                if not temp_free:
                    act.wait_ge(x_acc, e - 1)
                nc.scalar.activation(T[k % 2], xT[:, k, :], ACT.Square).then_inc(x_sq, 1)

            def norm_tile(e, k, weight):
                act.wait_ge(x_upd, e + 1)
                norm_high(k, weight)
                norm_square(e, k)

            act.wait_ge(ready0, 1)
            act.wait_ge(angle_ready, 1)
            nc.scalar.activation(sinT[:], sq[:, 1, :], ACT.Sin)
            nc.scalar.activation(sq[:, 3, :], sq[:, 1, :], ACT.Sin, scale=0.5).then_inc(sines_ready, 1)
            act.wait_ge(nw_full, 16)
            for k in range(KT):
                if k % 2 == 0:
                    act.wait_ge(bank_full, k + 1)
                    nc.scalar.activation(xT[:, k, :], bank[k % 4][:], ACT.Copy).then_inc(bank_free[k % 4], 1)
                    nc.scalar.drain()
                else:
                    act.wait_ge(x_odd, k // 2 + 1)
                norm_high(k, nw[:, k:k + 1])
                if k:
                    norm_square(k - 1, k - 1, temp_free=k <= 2)
                if k == 3:
                    for pos in (0, 2):
                        split_high(0, 0, 0, pos)
            norm_square(KT - 1, KT - 1)

            with act.Fori(0, DEPTH) as l:
                for n, word in enumerate(SEQUENCE):
                    kind, i = step_of(word)
                    nc.scalar.drain()
                    if n in SPLIT_AT:
                        split_high(l, *ahead(0, 0, SPLIT_AT[n]))
                    if word in UNIT:
                        pos = UNIT[word]
                        if kind == "ga":
                            split_high(l, *ahead(0, 0, pos + 1))
                        if kind in ("sq", "sk"):
                            act.wait_ge(swa_raw, l * 5 + (4 if kind == "sk" else i) + 1)
                            nc.scalar.activation(sqk[:] if kind == "sk" else sqr[:, i, :],
                                                 ct[:] if kind == "sk" else sq[:, i, :], ACT.Square).then_inc(swa_sq, 1)
                        elif kind == "cb":
                            act.wait_ge(y_val, l * 8 + i + 1)
                            nc.scalar.activation(yh[:, i, :], conv[i % 2][:], ACT.Copy).then_inc(y_hi, 1)
                        elif kind == "gr":
                            act.wait_ge(gr_scaled, l * 4 + i + 1)
                            nc.scalar.activation(ct[:], T[i % 2], ACT.Tanh, scale=0.5).then_inc(gr_tanh, 1)
                            if n in SPLIT_WITHIN:
                                split_high(l, *ahead(0, 0, SPLIT_WITHIN[n]))
                            act.wait_ge(y_val, l * 8 + 4 + i + 1)
                            nc.scalar.activation(yh[:, 4 + i, :], T[i % 2], ACT.Copy).then_inc(y_hi, 1)
                            nc.scalar.activation(mixed[:, 2 * i:2 * i + 2, :], zero_col.unsqueeze(2).broadcast_to([P, 2, SEQ]),
                                                 ACT.Copy)
                        elif word == "gq1":
                            nc.scalar.activation(attm[:], zero_col.unsqueeze(2).unsqueeze(3).broadcast_to([P, 2, TT, P]), ACT.Copy)
                    elif kind == "ZA":
                        act.wait_ge(z_biased, l * 2 + 2)
                        nc.scalar.activation(eb[:], gb[:], ACT.Abs)
                        nc.scalar.drain()
                        nc.scalar.activation(eb[:], eb[:], ACT.Exp, scale=-1.0)
                        nc.scalar.drain()
                        nc.scalar.activation(eb[:], eb[:], ACT.Ln, bias=one_col).then_inc(softplus_ready, 1)
                    elif kind == "ZB":
                        act.wait_ge(b_ready, l + 1)
                        nc.scalar.activation(eb[:], gb[:], ACT.Exp, scale=1.0 / 16)
                        nc.scalar.activation(kin[:], gb[:], ACT.Exp, scale=-1.0 / 16)
                        nc.scalar.drain()
                        nc.scalar.activation(gb[:], T3[:, 0:2, :], ACT.Exp, scale=-1.0 / 16).then_inc(gla_exps, 1)
                    elif kind == "VT":
                        b, free = filled(l, word)
                        nc.scalar.activation(vT[:, i].rearrange("p t n -> p (t n)"), b[:], ACT.Copy).then_inc(free, 1)
                        nc.scalar.drain().then_inc(vT_ready, 1)
                    elif kind == "KT":
                        b, free = filled(l, word)
                        nc.scalar.activation(kendT[:, i].rearrange("p t n -> p (t n)"), b[:], ACT.Copy).then_inc(free, 1)
                        nc.scalar.drain().then_inc(kendT_ready, 1)
                    elif kind == "GO":
                        b, free = filled(l, word)
                        nc.scalar.activation(yo[:, i, :], b[:], ACT.Copy).then_inc(free, 1)
                        nc.scalar.drain().then_inc(yo_ready, 1)
                        nc.scalar.activation(sqo[i][:], yo[:, i, :], ACT.Square).then_inc(yo_sq, 1)
                    elif kind == "QW":
                        act.wait_ge(stat_ready, l * 4 + 2)
                        for pair in QN_ORDER:
                            nc.scalar.activation(wide[pair][:], stat[:, 1, :].rearrange("p (t h) -> p t h", t=TT)
                                                 [:, :, 2 * pair:2 * pair + 2].unsqueeze(3).broadcast_to([P, TT, 2, SWA_DIM]),
                                                 ACT.Copy).then_inc(wide_ready, 1)
                    elif kind == "SC":
                        act.wait_ge(scores_ready, l * 8 + i + 1)
                        keys = slice(0, 2 * P) if i % TT else slice(P, 2 * P)
                        buf = i % 2
                        for h in range(4):
                            nc.scalar.activation(sm[buf][:, h, keys], sm[buf][:, h, keys], ACT.Exp,
                                                 bias=neg4[buf][:, h:h + 1], accum_out=sum4[buf][:, h:h + 1])
                        nc.scalar.activation(es4[buf], d4[buf], ACT.Exp).then_inc(exps_ready, 1)
                    elif kind == "SM":
                        act.wait_ge(den_ready, l * 8 + i + 1)
                        keys = slice(0, 2 * P) if i % TT else slice(P, 2 * P)
                        for h in range(4):
                            last = nc.scalar.activation(sm[i % 2][:, h, keys], sm[i % 2][:, h, keys], ACT.Copy,
                                                        scale=den4[i % 2][:, h:h + 1])
                        last.then_inc(probs_ready, 1)
                    elif kind == "PT":
                        for cur in ((0, 1) if i % TT else (1,)):
                            b, free = filled(l, word + ("cur" if cur else "prev"))
                            nc.scalar.activation(pT[:, cur].rearrange("p h c -> p (h c)"), b[:], ACT.Copy).then_inc(free, 1)
                            nc.scalar.drain().then_inc(pcur_ready if cur else pprev_ready, 1)
                    elif kind == "PV":
                        b, _ = filled(l, word)
                        kv, n = i // TT, i % TT
                        for odd in range(2):
                            r = slice(SWA_DIM * odd, SWA_DIM * (odd + 1))
                            last = nc.scalar.activation(
                                yh[r, 8 + 2 * kv:10 + 2 * kv, n * P:(n + 1) * P],
                                b[r, 2 * odd * P:(2 * odd + 2) * P].rearrange("p (j c) -> p j c", j=2), ACT.Copy)
                        last.then_inc(pv_hi, 1)

                def gates(g, final):
                    for pos in range(GATE_IT):
                        split_high(l, *ahead(G0, g, pos))
                        if pos % 8 < 4:
                            act.wait_ge(gate_scaled, l * 24 + g * 8 + (pos // 8 * 4 + pos % 4 + 1))
                            nc.scalar.activation(gt[:, pos % 4, :], gt[:, pos % 4, :], ACT.Tanh, scale=0.5).then_inc(gate_ready, 1)
                        elif final:
                            d = pos // 8 * 4 + pos % 4
                            act.wait_ge(mixed_done, l * 8 + d + 1)
                            nc.scalar.activation(yh[:, d, :], mixed[:, d, :], ACT.Copy, scale=0.5).then_inc(mx_hi, 1)

                with act.Fori(0, N_BRANCH - 1) as g:
                    gates(g, False)
                gates(N_BRANCH - 1, True)
                for pos in range(KT):
                    split_high(l, *ahead(O0, 0, pos))
                    norm_tile(l * 16 + (8 + pos), pos, nw[:, bass.ds(l * KT + (DEPTH * KT + pos), 1)])

                def mlp_quarter(q, final):
                    for pos in range(MLP_IT):
                        for which in (splits_in_last_quarter(l, pos) if final else [(l, *ahead(M0, q, pos))]):
                            split_high(*which)
                        if pos < 8:
                            a, free = done(l, M0, q, pos)
                            act.wait_ge(hid_ready, l * 32 + q * 8 + (pos - 1 + HID_CREDIT))
                            nc.scalar.activation(T[pos % 2], a[:], ACT.Relu).then_inc(free, 1)
                            nc.scalar.drain().then_inc(relu_ready, 1)
                            act.wait_ge(hid_val, l * 32 + q * 8 + (pos + 1))
                            nc.scalar.activation(yh[:, pos, :], T[pos % 2], ACT.Copy).then_inc(hid_hi, 1)
                        elif final:
                            k = pos - 8
                            norm_tile(l * 16 + (16 + k), k, nw[:, bass.ds(l * KT + (KT + k), 1)])

                with act.Fori(0, QUARTERS - 1) as q:
                    mlp_quarter(q, False)
                mlp_quarter(QUARTERS - 1, True)

        @block.vector
        def _(dve):
            V = nc.vector
            for s, n in ([(x, 1) for x in raw_free + acc_free + bank_free + [par_free]]
                         + [(hid_ready, HID_CREDIT), (x_upd, KT)]):
                dve.sem_inc(s, n)
            V.memset(one_col, 1.0)
            V.memset(zero_col, 0.0)
            V.drain().then_inc(ready0, 1)

            def filled(l, name, plain=False):
                f = FILL[name]
                fills = dve.to_reg(l * N_FILLS + (XF + f + 1))
                if plain:
                    dve.wait_ge(in_full, 16)
                dve.wait_ge(bank_full, fills)
                return bank[f % 4], bank_free[f % 4]

            def split_low(l, base, it, pos):
                dve.wait_ge(hi_done, l * UNITS + unit_index(base, it, pos) + (2 if base == 0 and pos == 0 else 1))
                V.tensor_tensor(split_view(wl, base, pos), raw_view(base, pos), split_view(wh, base, pos).bitcast(f32),
                                ALU.subtract).then_inc(lo_done, 2 if base == 0 and pos == 0 else 1)
                if slab_ends(base, pos) or (base == 0 and pos == 0):
                    V.drain().then_inc(raw_free[slab_slot(base, pos)], 1)

            def done(l, base, it, pos):
                dve.wait_ge(unit_done, l * UNITS + unit_index(base, it, pos) + 1 + UNIT_CREDIT)
                return acc[(base + pos) % 4], acc_free[(base + pos) % 4]

            def norm_low(e, k, weight):
                dve.wait_ge(u_hi, e + 1)
                V.scalar_tensor_tensor(out=ul[:, k, :], in0=xT[:, k, :], scalar=weight, in1=uh[:, k, :].bitcast(f32),
                                       op0=ALU.mult, op1=ALU.subtract).then_inc(u_ready, 1)

            def norm_sum(e, k):
                dve.wait_ge(x_sq, e + 1)
                if k == 0:
                    V.tensor_copy(nacc[:], T[0]).then_inc(x_acc, 1)
                else:
                    V.tensor_tensor(nacc[:], nacc[:], T[k % 2], ALU.add).then_inc(x_acc, 1)

            def scaled_q(l, i):
                a, free = done(l, 0, 0, UNIT[f"gq{i}"])
                V.scalar_tensor_tensor(out=gq[:, i, :], in0=a[:], scalar=GLA_DK ** -0.5, in1=rs[:],
                                       op0=ALU.mult, op1=ALU.mult).then_inc(free, 1)

            def conv_low(l, i):
                dve.wait_ge(y_hi, l * 8 + i + 1)
                V.tensor_tensor(yl[:, i, :], conv[i % 2][:], yh[:, i, :].bitcast(f32), ALU.subtract).then_inc(yconv_ready, 1)

            def gla_low(l, i):
                dve.wait_ge(y_hi, l * 8 + 4 + i + 1)
                V.tensor_tensor(yl[:, 4 + i, :], T[i % 2], yh[:, 4 + i, :].bitcast(f32), ALU.subtract).then_inc(ygla_ready, 1)

            def rsqrt(l, name, columns, n, result, square=False):
                b, free = filled(l, name)
                a, y, t = (stat[:, j, 0:columns] for j in (0, result, 2))
                bits = stat_i[:, 0:columns]
                V.tensor_scalar(a, b[:, 0:columns], 1.0 / n, EPS, ALU.mult, ALU.add).then_inc(free, 1)
                V.drain()
                V.tensor_scalar(bits, a.bitcast(i32), 1, None, ALU.logical_shift_right)
                V.drain()
                V.tensor_scalar(y.bitcast(i32), bits, -1, 0x5F3759DF, ALU.mult, ALU.add)
                V.drain()
                for _ in range(3):
                    V.tensor_tensor(t, a, y, ALU.mult)
                    V.drain()
                    V.scalar_tensor_tensor(out=t, in0=t, scalar=-0.5, in1=y, op0=ALU.mult, op1=ALU.mult)
                    V.drain()
                    V.scalar_tensor_tensor(out=y, in0=t, scalar=1.5, in1=y, op0=ALU.add, op1=ALU.mult)
                    V.drain()
                if square:
                    V.tensor_tensor(y, y, y, ALU.mult)
                    V.drain()
                V.drain().then_inc(stat_ready, 1)

            dve.wait_ge(in_full, 16)
            dve.wait_ge(pos_full, 16)
            V.tensor_copy(sq[:, 2, :], pos_i[:])
            V.drain()
            V.tensor_scalar(sq[:, 1, :], sq[:, 2, :], invf, None, ALU.mult)
            V.drain()
            V.tensor_scalar(sq[:, 2, :], sq[:, 1, :], 1.0 / TWO_PI, ROUND, ALU.mult, ALU.add)
            V.drain()
            V.tensor_scalar(sq[:, 3, :], sq[:, 2, :], -ROUND, None, ALU.add)
            V.drain()
            for part in (PI_1, PI_2, PI_3):
                V.scalar_tensor_tensor(out=sq[:, 1, :], in0=sq[:, 3, :], scalar=-part, in1=sq[:, 1, :],
                                       op0=ALU.mult, op1=ALU.add)
                V.drain()
            V.tensor_scalar(sq[:, 1, :], sq[:, 1, :], 3.1415925, -3.1415925, ALU.min, ALU.max).then_inc(angle_ready, 1)
            dve.wait_ge(sines_ready, 1)
            V.tensor_tensor(cosT[:], sq[:, 3, :], sq[:, 3, :], ALU.mult)
            V.tensor_scalar(sinT[:], sinT[:], sign, None, ALU.mult)
            V.drain()
            V.tensor_scalar(cosT[:], cosT[:], -2.0, 1.0, ALU.mult, ALU.add)
            dve.wait_ge(nw_full, 16)
            for k in range(KT + 1):
                V.drain()
                if k % 2:
                    dve.wait_ge(bank_full, k + 1)
                    V.tensor_copy(xT[:, k, :], bank[k % 4][:]).then_inc(bank_free[k % 4], 1)
                    V.drain().then_inc(x_odd, 1)
                if k:
                    norm_low(k - 1, k - 1, nw[:, k - 1:k])
                if k >= 2:
                    norm_sum(k - 2, k - 2)
                if k == 5:
                    for pos in (0, 2):
                        split_low(0, 0, 0, pos)
            V.drain()
            norm_sum(KT - 1, KT - 1)
            dve.wait_ge(masks_full, 16)
            dve.wait_ge(gm_full, 16)

            with dve.Fori(0, DEPTH) as l:
                dve.wait_ge(par_full, l * 32 + 32)
                V.tensor_scalar(qn8, par[:, PC["qn"]:PC["qn"] + 1], SWA_DIM ** -0.5, None, ALU.mult)
                for n, word in enumerate(SEQUENCE):
                    kind, i = step_of(word)
                    V.drain()
                    if n in SPLIT_AT:
                        split_low(l, *ahead(0, 0, SPLIT_AT[n]))
                        V.drain()
                    if word in UNIT:
                        pos = UNIT[word]
                        if kind == "ga":
                            V.drain().then_inc(acc_free[1], 1)
                            split_low(l, *ahead(0, 0, pos + 1))
                        elif kind == "gq" and i:
                            scaled_q(l, i)
                        elif kind == "gk":
                            a, free = done(l, 0, 0, pos)
                            V.tensor_tensor(gk[:, i, :], a[:], rs[:], ALU.mult).then_inc(free, 1)
                        elif kind == "gv":
                            if i:
                                dve.wait_ge(bank_full, l * N_FILLS + XF + FILL["VS0" if i == 1 else f"VT{i - 2}"] + 1)
                            a, free = done(l, 0, 0, pos)
                            V.tensor_tensor(vtmp[:, (i + 1) % 2, :], a[:], rs[:], ALU.mult).then_inc(free, 1)
                            V.drain().then_inc(gv_ready, 1)
                        elif kind == "sv":
                            a, free = done(l, 0, 0, pos)
                            V.tensor_tensor(vtmp[:, 0, :], a[:], rs[:], ALU.mult).then_inc(free, 1)
                            V.drain().then_inc(sv_ready, 1)
                        elif kind in ("sq", "sk"):
                            a, free = done(l, 0, 0, pos)
                            V.tensor_tensor(ct[:] if kind == "sk" else sq[:, i, :], a[:], rs[:], ALU.mult).then_inc(free, 1)
                            V.drain().then_inc(swa_raw, 1)
                        elif kind == "cx":
                            a, free = done(l, 0, 0, pos)
                            V.tensor_tensor(cu[:, i, :], a[:], rs_sq, ALU.mult).then_inc(free, 1)
                        elif kind == "cc":
                            a, free = done(l, 0, 0, pos)
                            V.tensor_tensor(cu[:, i, :], a[:], cu[:, i, :], ALU.mult).then_inc(free, 1)
                        elif kind == "cb":
                            w = [par[:, PC["cw"] + 4 * k + i:PC["cw"] + 4 * k + i + 1] for k in range(3)]
                            y = conv[i % 2]
                            if i:
                                conv_low(l, i - 1)
                            V.tensor_scalar(y[:], cu[:, i, :], w[2], par[:, PC["cb"] + i:PC["cb"] + i + 1], ALU.mult, ALU.add)
                            V.drain()
                            for back in (1, 2):
                                V.scalar_tensor_tensor(out=y[:, back:], in0=cu[:, i, 0:SEQ - back], scalar=w[2 - back],
                                                       in1=y[:, back:], op0=ALU.mult, op1=ALU.add)
                                V.drain()
                            V.tensor_tensor(y[:], y[:], rs[:], ALU.mult)
                            V.drain()
                            a, free = done(l, 0, 0, pos)
                            V.tensor_tensor(y[:], a[:], y[:], ALU.mult).then_inc(free, 1)
                            V.drain().then_inc(y_val, 1)
                        elif kind == "gr":
                            t = T[i % 2]
                            if i == 0:
                                conv_low(l, 3)
                            a, free = done(l, 0, 0, pos)
                            V.tensor_tensor(t, a[:], rs[:], ALU.mult).then_inc(free, 1)
                            V.drain().then_inc(gr_scaled, 1)
                            if i:
                                gla_low(l, i - 1)
                            if n in SPLIT_WITHIN:
                                split_low(l, *ahead(0, 0, SPLIT_WITHIN[n]))
                            dve.wait_ge(gr_tanh, l * 4 + i + 1)
                            V.scalar_tensor_tensor(out=t, in0=ct[:], scalar=1.0, in1=t, op0=ALU.add, op1=ALU.mult)
                            V.drain()
                            V.scalar_tensor_tensor(out=t, in0=t, scalar=0.5, in1=yo[:, i, :], op0=ALU.mult, op1=ALU.mult)
                            V.drain().then_inc(y_val, 1)
                    elif kind == "NSUM":
                        rsqrt(l, word, TT, D_MODEL, 1)
                    elif kind == "NROW":
                        b, free = filled(l, word)
                        V.tensor_copy(rs[:], b[:]).then_inc(free, 1)
                        V.drain()
                        a, free = done(l, 0, 0, UNIT["ga"])
                        V.tensor_tensor(gaT[0:GLA_RANK, :], a[0:GLA_RANK, :], rs[0:GLA_RANK, :], ALU.mult).then_inc(free, 1)
                        V.drain().then_inc(ga_ready, 1)
                        scaled_q(l, 0)
                        V.tensor_tensor(rs_sq, rs[:], rs[:], ALU.mult)
                    elif kind == "ZA":
                        for pair in range(2):
                            b, free = filled(l, word + "ab"[pair])
                            V.tensor_scalar(gb[:, pair, :], b[:], par[:, PC["ba"] + pair:PC["ba"] + pair + 1], None,
                                            ALU.add).then_inc(free, 1)
                            V.drain().then_inc(z_biased, 1)
                    elif kind == "ZB":
                        dve.wait_ge(softplus_ready, l + 1)
                        V.scalar_tensor_tensor(out=kin[:], in0=gb[:], scalar=0.0, in1=eb[:], op0=ALU.min, op1=ALU.subtract)
                        V.drain()
                        for pair in range(2):
                            V.tensor_tensor_scan(gb[:, pair, :], scanm, kin[:, pair, :], 0.0, ALU.mult, ALU.add)
                        V.drain()
                        bc = gb[:].rearrange("p h (c n) -> p (h c) n", n=GLA_CHUNK)
                        V.tensor_tensor(T3[:, 0:2, :].rearrange("p h (c n) -> p (h c) n", n=GLA_CHUNK), bc,
                                        bc[:, :, GLA_CHUNK - 1:GLA_CHUNK].broadcast_to([P, 2 * CHUNKS, GLA_CHUNK]),
                                        ALU.subtract).then_inc(b_ready, 1)
                    elif kind == "X":
                        dve.wait_ge(gla_exps, l + 1)
                        V.tensor_tensor(gq[:, i, :], gq[:, i, :], eb[:, i, :], ALU.mult)
                        V.tensor_tensor(kin[:, i, :], gk[:, i, :], kin[:, i, :], ALU.mult)
                        V.drain()
                        V.tensor_tensor(gk[:, i, :], gk[:, i, :], gb[:, i, :], ALU.mult).then_inc(gla_qk, 1)
                    elif kind == "ATT":
                        if i >= 2:
                            dve.wait_ge(bank_full, l * N_FILLS + XF + FILL[f"GO{i - 2}"] + 1)
                        b, free = filled(l, word, True)
                        for t in range(TT):
                            last = V.copy_predicated(attm[:, i % 2, t, :], gm[:], b[:, t * P:(t + 1) * P])
                        last.then_inc(free, 1)
                        V.drain().then_inc(att_ready, 1)
                    elif kind == "KV":
                        be, free_e = filled(l, word + "a")
                        bo, free_o = filled(l, word + "b")
                        V.tensor_copy(S[:, i, 0, :], be[:, 0:P])
                        for c in range(1, CHUNKS - 1):
                            V.drain()
                            b = (be, bo)[c % 2]
                            last_c = GLA_CHUNK * (c + 1) - 1
                            V.scalar_tensor_tensor(out=S[:, i, c, :], in0=S[:, i, c - 1, :], scalar=eb[:, i, last_c:last_c + 1],
                                                   in1=b[:, c // 2 * P:(c // 2 + 1) * P], op0=ALU.mult, op1=ALU.add)
                        V.drain().then_inc(free_e, 1)
                        V.drain().then_inc(free_o, 1)
                        V.drain().then_inc(states_ready, 1)
                    elif kind == "QSUM":
                        rsqrt(l, word, TT * HEADS_Q, SWA_DIM, 1)
                    elif kind == "OSUM":
                        rsqrt(l, word, TT * GLA_HEADS, GLA_DV, 3)
                    elif kind == "QN":
                        t = ct[:] if i == 4 else sq[:, i, :]
                        w = par[:, PC["kn"]:PC["kn"] + 1] if i == 4 else qn8
                        b, free = filled(l, word)
                        V.scalar_tensor_tensor(out=t, in0=t, scalar=w, in1=b[:], op0=ALU.mult, op1=ALU.mult).then_inc(free, 1)
                        V.drain()
                        V.stream_shuffle(T[1], t, ROPE_SWAP)
                        V.drain()
                        V.tensor_tensor(T[1], T[1], sinT[:], ALU.mult)
                        V.tensor_tensor(t, t, cosT[:], ALU.mult)
                        V.drain()
                        if i < 4:
                            V.tensor_tensor(t, t, T[1], ALU.add).then_inc(swa_roped, 1)
                        else:
                            for kv in range(2):
                                src = slice(SWA_DIM * kv, SWA_DIM * (kv + 1))
                                for half in range(2):
                                    V.tensor_tensor(kd[SWA_DIM * half:SWA_DIM * (half + 1), kv, :], ct[src, :],
                                                    T[1][src, :], ALU.add)
                            V.drain().then_inc(swa_roped, 1)
                    elif kind == "ON":
                        dve.wait_ge(yo_ready, l * 4 + i + 1)
                        b, free = filled(l, word)
                        V.scalar_tensor_tensor(out=yo[:, i, :], in0=yo[:, i, :], scalar=par[:, PC["on"]:PC["on"] + 1],
                                               in1=b[:], op0=ALU.mult, op1=ALU.mult).then_inc(free, 1)
                    elif kind == "VS":
                        b, free = filled(l, word)
                        bv = b[:].rearrange("p (t k d) -> p t k d", t=TT, k=2)
                        for kv in range(2):
                            for half in range(2):
                                last = V.tensor_copy(vd[:, kv, :, half, :], bv[:, :, kv, :])
                        last.then_inc(free, 1)
                        V.drain().then_inc(vs_ready, 1)
                    elif kind == "SC":
                        first, buf = 0 if i % TT else P, i % 2
                        if i >= 2:
                            dve.wait_ge(bank_full, l * N_FILLS + XF + FILL[f"PT{i - 2}cur"] + 1)
                        for odd in range(2):
                            b, free = filled(l, word + "ab"[odd])
                            V.tensor_tensor(sm[buf][:, 2 * odd:2 * odd + 2, first:],
                                            b[:].rearrange("p (j c) -> p j c", j=2)[:, :, first:],
                                            swam.unsqueeze(1).broadcast_to([P, 2, 2 * P])[:, :, first:], ALU.add).then_inc(free, 1)
                        V.drain()
                        V.tensor_reduce(m4, sm[buf][:, :, first:], AX.X, ALU.max)
                        V.drain()
                        sink = par[:, PC["sink"] + i // TT * 4:PC["sink"] + i // TT * 4 + 4]
                        V.tensor_tensor(m4, m4, sink, ALU.max)
                        V.drain()
                        V.tensor_scalar(neg4[buf], m4, -1.0, None, ALU.mult)
                        V.tensor_tensor(d4[buf], sink, m4, ALU.subtract)
                        V.drain().then_inc(scores_ready, 1)
                    elif kind == "SM":
                        dve.wait_ge(exps_ready, l * 8 + i + 1)
                        V.tensor_tensor(den4[i % 2], sum4[i % 2], es4[i % 2], ALU.add)
                        V.drain()
                        V.reciprocal(den4[i % 2], den4[i % 2])
                        V.drain().then_inc(den_ready, 1)
                    elif kind == "PV":
                        b, free = filled(l, word)
                        kv, n = i // TT, i % TT
                        dve.wait_ge(pv_hi, l * 8 + i + 1)
                        for odd in range(2):
                            r = slice(SWA_DIM * odd, SWA_DIM * (odd + 1))
                            at_y = (r, slice(8 + 2 * kv, 10 + 2 * kv), slice(n * P, (n + 1) * P))
                            last = V.tensor_tensor(yl[at_y], b[r, 2 * odd * P:(2 * odd + 2) * P].rearrange("p (j c) -> p j c", j=2),
                                                   yh[at_y].bitcast(f32), ALU.subtract)
                        last.then_inc(free, 1)
                        V.drain().then_inc(yswa_ready, 1)
                V.drain().then_inc(par_free, 1)
                gla_low(l, 3)

                def mixed_low(d):
                    dve.wait_ge(mx_hi, l * 8 + d + 1)
                    V.scalar_tensor_tensor(out=yl[:, d, :], in0=mixed[:, d, :], scalar=0.5, in1=yh[:, d, :].bitcast(f32),
                                           op0=ALU.mult, op1=ALU.subtract).then_inc(mx_ready, 1)

                def gates(g, final):
                    for pos in range(GATE_IT):
                        d = pos // 8 * 4 + pos % 4
                        V.drain()
                        late = final and pos % 8 >= 4
                        if not late:
                            split_low(l, *ahead(G0, g, pos))
                        if pos % 8 < 4:
                            if final and pos == 8:
                                mixed_low(d - 1)
                            a, free = done(l, G0, g, pos)
                            V.tensor_tensor(gt[:, pos % 4, :], a[:], rs[:], ALU.mult).then_inc(free, 1)
                            V.drain().then_inc(gate_scaled, 1)
                        else:
                            dve.wait_ge(gate_ready, l * 24 + g * 8 + (d + 1))
                            a, free = done(l, G0, g, pos)
                            V.scalar_tensor_tensor(out=T[pos % 2], in0=gt[:, pos % 4, :], scalar=1.0, in1=a[:],
                                                   op0=ALU.add, op1=ALU.mult).then_inc(free, 1)
                            V.drain()
                            V.tensor_tensor(mixed[:, d, :], mixed[:, d, :], T[pos % 2], ALU.add)
                            if final:
                                V.drain().then_inc(mixed_done, 1)
                                if pos % 4:
                                    mixed_low(d - 1)
                                split_low(l, *ahead(G0, g, pos))

                with dve.Fori(0, N_BRANCH - 1) as g:
                    gates(g, False)
                gates(N_BRANCH - 1, True)
                mixed_low(KT - 1)
                for pos in range(KT):
                    V.drain()
                    split_low(l, *ahead(O0, 0, pos))
                    a, free = done(l, O0, 0, pos)
                    V.tensor_tensor(xT[:, pos, :], xT[:, pos, :], a[:], ALU.add).then_inc(free, 1)
                    V.drain().then_inc(x_upd, 1)
                    norm_low(l * 16 + (8 + pos), pos, nw[:, bass.ds(l * KT + (DEPTH * KT + pos), 1)])
                    norm_sum(l * 16 + (8 + pos), pos)

                def mlp_quarter(q, first=False, final=False):
                    for pos in range(MLP_IT):
                        V.drain()
                        for which in (splits_in_last_quarter(l, pos) if final else [(l, *ahead(M0, q, pos))]):
                            split_low(*which)
                        if pos < 8:
                            t = T[pos % 2]
                            dve.wait_ge(relu_ready, l * 32 + q * 8 + (pos + 1))
                            V.tensor_tensor(t, t, t, ALU.mult).then_inc(hid_val, 1)
                            dve.wait_ge(hid_hi, l * 32 + q * 8 + (pos + 1))
                            V.tensor_tensor(yl[:, pos, :], t, yh[:, pos, :].bitcast(f32), ALU.subtract).then_inc(hid_ready, 1)
                            if first and pos == 1:
                                rsqrt(l, "NSUM2", TT, D_MODEL, 1, square=True)
                            elif first and pos == 3:
                                b, free = filled(l, "NROW2")
                                V.tensor_copy(rs2[:], b[:]).then_inc(free, 1)
                        else:
                            k = pos - 8
                            a, free = done(l, M0, q, pos)
                            V.tensor_tensor(T[2], a[:], rs2[:], ALU.mult).then_inc(free, 1)
                            V.drain()
                            V.tensor_tensor(xT[:, k, :], xT[:, k, :], T[2], ALU.add)
                            if final:
                                V.drain().then_inc(x_upd, 1)
                                norm_low(l * 16 + (16 + k), k, nw[:, bass.ds(l * KT + (KT + k), 1)])
                                norm_sum(l * 16 + (16 + k), k)

                mlp_quarter(0, first=True)
                with dve.Fori(1, QUARTERS - 1) as q:
                    mlp_quarter(q)
                mlp_quarter(QUARTERS - 1, final=True)
            for e in range(2 * TT):
                t, half = e // 2, e % 2
                dve.wait_ge(bank_full, DEPTH * N_FILLS + XF + e + 1)
                V.tensor_copy(x_tok[:, t, half * 512:(half + 1) * 512], bank[e % 4][:]).then_inc(bank_free[e % 4], 1)
                V.drain().then_inc(out_copied, 1)


def constants():
    c = np.zeros((P, N_CONST), np.float32)
    p = np.arange(P)
    c[p, CC["ident"] + p] = 1.0
    c[:, CC["ones"]] = 1.0
    c[:, CC["blk"]:CC["blk"] + 2] = p[:, None] // SWA_DIM == np.arange(2)[None, :]
    c[:, CC["sign"]] = np.where(p % SWA_DIM < ROPE_HALF, -1.0, 1.0)
    half = ROPE_HALF
    c[:, CC["scan"]:CC["scan"] + SEQ] = np.arange(SEQ) % GLA_CHUNK != 0
    key = np.arange(2 * P)[None, :]
    c[:, CC["swam"]:CC["swam"] + 2 * P] = np.where((key > p[:, None]) & (key <= p[:, None] + P), 0.0, -3.0e38)
    freq = np.float32(500000.0) ** (-np.arange(0, 2 * half, 2, dtype=np.float32) / np.float32(2 * half))
    c[:, CC["invf"]] = np.where(p % SWA_DIM < 2 * half, freq[p % half], 0.0)
    g = (p[None, :] >= p[:, None]) & (p[None, :] // GLA_CHUNK == p[:, None] // GLA_CHUNK)
    return c, g.astype(np.int32)


def kernel(**inputs):
    import concourse.bacc as _bacc
    from concourse.bass_utils import run_bass_kernel_spmd as _run

    a = {k: np.asarray(v) for k, v in inputs.items()}

    def cols(w):
        return w.reshape(DEPTH, -1, P).transpose(0, 2, 1)

    sinks = a["sinks"].reshape(DEPTH, SWA_KV, 2, 2).transpose(0, 1, 3, 2).reshape(DEPTH, 1, SWA_HEADS)
    params = np.concatenate([
        cols(a["conv_w"].reshape(DEPTH, -1)), cols(a["conv_b"]),
        cols(a["gla_ba"]), cols(a["gla_onorm_w"]), cols(np.tile(a["q_norm_w"], (1, 2))),
        cols(np.tile(a["k_norm_w"], (1, 2))), np.broadcast_to(sinks, (DEPTH, P, SWA_HEADS))], axis=2)
    norms = np.concatenate([a["norm1_w"], a["norm2_w"]]).reshape(2 * DEPTH * KT, P).T
    consts, gmask = constants()
    feed = dict(x=a["x"], positions=a["positions"][0], params=params, w_in=a["w_in"], gla_wa2=a["gla_wa2"],
                w_branch=a["w_branch"], w_o=a["w_o"], w_up=a["w_up"], w_down=a["w_down"],
                norms=norms, consts=consts, gmask=gmask)
    nc = _bacc.Bacc("TRN2", target_bir_lowering=False, num_devices=1)
    arrays, args = {}, []
    for name, value in feed.items():
        value = np.ascontiguousarray(value)
        arrays[f"in_{name}_dram"] = value
        args.append(nc.dram_tensor(f"in_{name}_dram", value.shape, mybir.dt.from_np(value.dtype), kind="ExternalInput").ap())
    args.append(nc.dram_tensor("out_0_dram", (1, SEQ, D_MODEL), mybir.dt.float32, kind="ExternalOutput").ap())
    hybrid_trunk(nc, *args)
    r = _run(nc, [arrays], core_ids=[0])
    return r.results[0]["out_0_dram"]
```
